# Optimizing a Trainium2 kernel written in Bass

```python
import math
import jax, jax.numpy as jnp
from jax import lax
import numpy as np

D_MODEL = 1024
BATCH = 1
SEQ = 512
DEPTH = 1

D_MIX = D_MODEL
MOBA_HEADS = 8
MOBA_HEAD_DIM = 64
D_MOBA = MOBA_HEADS * MOBA_HEAD_DIM
GMLP_GROUPS = 8
GMLP_GROUP_DIM = 64
D_GMLP = GMLP_GROUPS * GMLP_GROUP_DIM
D_IN_PROJ = 3 * D_MOBA + 2 * D_GMLP

MOBA_BLOCK = 256
MOBA_TOPK = 3
Q_CHUNK = 128
GMLP_CHUNK = 128

NUM_BUCKETS = 32
REL_MAX_DISTANCE = 128

D_FF = -(-(8 * D_MODEL) // (3 * 256)) * 256
EPS = 1e-6
NEG = -1e9

kernel_name = 'hybrid_moba_chunked_gmlp_block'

def rms_norm(x, g):
    xf = x.astype(jnp.float32)
    y = xf * lax.rsqrt(jnp.mean(xf * xf, axis=-1, keepdims=True) + EPS)
    return (y * g.astype(jnp.float32)).astype(x.dtype)

def layer_norm(x, g, b):
    xf = x.astype(jnp.float32)
    mu = jnp.mean(xf, axis=-1, keepdims=True)
    var = jnp.mean(jnp.square(xf - mu), axis=-1, keepdims=True)
    y = (xf - mu) * lax.rsqrt(var + EPS)
    return (y * g.astype(jnp.float32) + b.astype(jnp.float32)).astype(x.dtype)

def t5_bucket(dist):
    n = jnp.maximum(dist, 0)
    max_exact = NUM_BUCKETS // 2
    nf = jnp.maximum(n, max_exact).astype(jnp.float32)
    large = max_exact + (jnp.log(nf / max_exact) / math.log(REL_MAX_DISTANCE / max_exact)
                         * (NUM_BUCKETS - max_exact)).astype(jnp.int32)
    large = jnp.minimum(large, NUM_BUCKETS - 1)
    return jnp.where(n < max_exact, n, large)

def moba_attention(q, k, v, rel_bias):
    B, S, H, D = q.shape
    S_pad = -(-S // MOBA_BLOCK) * MOBA_BLOCK
    pad = S_pad - S
    q, k, v = [jnp.pad(t, ((0, 0), (0, pad), (0, 0), (0, 0))).transpose(0, 2, 1, 3)
               for t in (q, k, v)]
    NB = S_pad // MOBA_BLOCK
    k_blk = k.reshape(B, H, NB, MOBA_BLOCK, D)
    v_blk = v.reshape(B, H, NB, MOBA_BLOCK, D)
    k_mean = jnp.mean(k_blk.astype(jnp.float32), axis=3)
    gate = jnp.einsum('bhsd,bhnd->bhsn', q.astype(jnp.float32), k_mean)
    q_block = jnp.arange(S_pad) // MOBA_BLOCK
    past = jnp.arange(NB)[None, :] < q_block[:, None]
    gate = jnp.where(past[None, None], gate, NEG)
    topk = min(MOBA_TOPK, NB)
    _, top_idx = lax.top_k(gate, topk)
    valid = jnp.arange(topk)[None, :] < q_block[:, None]
    bias_hb = rel_bias.T.astype(jnp.float32)
    NC = S_pad // Q_CHUNK
    scale = D ** -0.5
    h_ix = jnp.arange(H)[:, None, None]
    l_idx = jnp.arange(MOBA_BLOCK)

    def step(idx):
        b, c = idx
        q0 = c * Q_CHUNK
        q_c = lax.dynamic_slice(q, (b, 0, q0, 0), (1, H, Q_CHUNK, D))[0]
        sel = lax.dynamic_slice(top_idx, (b, 0, q0, 0), (1, H, Q_CHUNK, topk))[0]
        ok = lax.dynamic_slice(valid, (q0, 0), (Q_CHUNK, topk))
        kb = k_blk[b]
        vb = v_blk[b]
        k_sel = kb[h_ix, sel]
        v_sel = vb[h_ix, sel]
        own = q0 // MOBA_BLOCK
        k_own = lax.dynamic_index_in_dim(kb, own, axis=1, keepdims=False)
        v_own = lax.dynamic_index_in_dim(vb, own, axis=1, keepdims=False)
        q_pos = q0 + jnp.arange(Q_CHUNK)
        pos_sel = sel[..., None] * MOBA_BLOCK + l_idx
        dist_sel = q_pos[None, :, None, None] - pos_sel
        b_sel = bias_hb[h_ix[..., None], t5_bucket(dist_sel)]
        dist_own = q_pos[:, None] - (own * MOBA_BLOCK + l_idx)[None, :]
        b_own = bias_hb[:, t5_bucket(dist_own)]
        l_sel = jnp.einsum('hqd,hqkld->hqkl', q_c, k_sel).astype(jnp.float32) * scale + b_sel
        l_sel = jnp.where(ok[None, :, :, None], l_sel, NEG)
        l_own = jnp.einsum('hqd,hld->hql', q_c, k_own).astype(jnp.float32) * scale + b_own
        l_own = jnp.where((dist_own >= 0)[None], l_own, NEG)
        logits = jnp.concatenate([l_sel.reshape(H, Q_CHUNK, topk * MOBA_BLOCK), l_own], axis=-1)
        p = jax.nn.softmax(logits, axis=-1).astype(v.dtype)
        p_sel = p[..., :topk * MOBA_BLOCK].reshape(H, Q_CHUNK, topk, MOBA_BLOCK)
        p_own = p[..., topk * MOBA_BLOCK:]
        return (jnp.einsum('hqkl,hqkld->hqd', p_sel, v_sel)
                + jnp.einsum('hql,hld->hqd', p_own, v_own))

    b_ids = jnp.repeat(jnp.arange(B), NC)
    c_ids = jnp.tile(jnp.arange(NC), B)
    out = lax.map(step, (b_ids, c_ids))
    out = out.reshape(B, NC, H, Q_CHUNK, D).transpose(0, 1, 3, 2, 4).reshape(B, S_pad, H * D)
    return out[:, :S]

def chunked_gmlp(u, z, ln_g, ln_b, w_spatial, b_spatial):
    B, S, _ = z.shape
    u = jax.nn.gelu(u)
    z = layer_norm(jax.nn.gelu(z), ln_g, ln_b)
    n_ch = S // GMLP_CHUNK
    z = z.reshape(B, n_ch, GMLP_CHUNK, GMLP_GROUPS, GMLP_GROUP_DIM)
    causal = jnp.tril(jnp.ones((GMLP_CHUNK, GMLP_CHUNK), dtype=z.dtype))
    w = w_spatial.astype(z.dtype) * causal
    s = jnp.einsum('gts,bcsgd->bctgd', w, z) + b_spatial.T.astype(z.dtype)[:, :, None]
    return u * s.reshape(B, S, D_GMLP)

def setup_inputs(seed: int = 0) -> dict:
    key = jax.random.key(seed)
    ks = jax.random.split(key, 16)

    def nrm(k, shape, scale):
        return jax.random.normal(k, shape, jnp.float32) * scale

    return {
        'x': nrm(ks[0], (BATCH, SEQ, D_MODEL), 1.0),
        'rel_bias': nrm(ks[1], (NUM_BUCKETS, MOBA_HEADS), 0.3),
        'norm_mix': 1.0 + nrm(ks[2], (DEPTH, D_MODEL), 0.05),
        'w_in': nrm(ks[3], (DEPTH, D_MODEL, D_IN_PROJ), D_MODEL ** -0.5),
        'gmlp_ln_g': 1.0 + nrm(ks[4], (DEPTH, D_GMLP), 0.05),
        'gmlp_ln_b': nrm(ks[5], (DEPTH, D_GMLP), 0.02),
        'w_spatial': nrm(ks[6], (DEPTH, GMLP_GROUPS, GMLP_CHUNK, GMLP_CHUNK), GMLP_CHUNK ** -0.5),
        'b_spatial': 1.0 + nrm(ks[7], (DEPTH, GMLP_GROUPS, GMLP_CHUNK), 0.1),
        'out_norm_b': 1.0 + nrm(ks[8], (DEPTH, D_MOBA), 0.05),
        'out_norm_a': 1.0 + nrm(ks[9], (DEPTH, D_GMLP), 0.05),
        'w_out': nrm(ks[10], (DEPTH, D_MIX, D_MODEL), D_MIX ** -0.5),
        'norm_ffn': 1.0 + nrm(ks[11], (DEPTH, D_MODEL), 0.05),
        'w_gate': nrm(ks[12], (DEPTH, D_MODEL, D_FF), D_MODEL ** -0.5),
        'w_up': nrm(ks[13], (DEPTH, D_MODEL, D_FF), D_MODEL ** -0.5),
        'w_down': nrm(ks[14], (DEPTH, D_FF, D_MODEL), D_FF ** -0.5),
        'norm_final': 1.0 + nrm(ks[15], (D_MODEL,), 0.05),
    }

def reference(x, rel_bias, norm_mix, w_in, gmlp_ln_g, gmlp_ln_b, w_spatial, b_spatial,
              out_norm_b, out_norm_a, w_out, norm_ffn, w_gate, w_up, w_down, norm_final):
    B, S, _ = x.shape
    for l in range(DEPTH):
        h = rms_norm(x, norm_mix[l])
        proj = h @ w_in[l]
        q, k, v, u, z = jnp.split(
            proj, [D_MOBA, 2 * D_MOBA, 3 * D_MOBA, 3 * D_MOBA + D_GMLP], axis=-1)
        shp = (B, S, MOBA_HEADS, MOBA_HEAD_DIM)
        y_b = moba_attention(q.reshape(shp), k.reshape(shp), v.reshape(shp), rel_bias)
        y_a = chunked_gmlp(u, z, gmlp_ln_g[l], gmlp_ln_b[l], w_spatial[l], b_spatial[l])
        y = jnp.concatenate([rms_norm(y_b, out_norm_b[l]), rms_norm(y_a, out_norm_a[l])], axis=-1)
        x = x + y @ w_out[l]
        h = rms_norm(x, norm_ffn[l])
        x = x + (jax.nn.silu(h @ w_gate[l]) * (h @ w_up[l])) @ w_down[l]
    return rms_norm(x, norm_final)


_drawn_inputs = setup_inputs


def setup_inputs(seed=0):
    import zlib

    import numpy as np

    out = dict(_drawn_inputs(seed))
    spreads = {}
    factors = {'gmlp_ln_g': 3.917, 'gmlp_ln_b': 21.745}
    for name, (base, spread) in spreads.items():
        noise = np.random.default_rng([zlib.crc32(name.encode()), seed]).standard_normal(out[name].shape)
        drawn = base * np.exp(spread * noise) if base else spread * noise
        out[name] = __import__('jax').numpy.asarray(drawn.astype(out[name].dtype))
    for name, factor in factors.items():
        out[name] = (out[name] * factor).astype(out[name].dtype)
    return out
```

```python
from contextlib import ExitStack

import numpy as np

import concourse.bass as bass
from concourse import mybir

P = 128
D = 1024
SEQ = 512
HEADS = 8
HD = 64
GROUPS = 8
GD = 64
HALF = 512
D_FF = 2816
BUCKETS = 32
MAX_DISTANCE = 128
EPS = 1e-6
NEG = -1e9
TT = SEQ // P
KT = D // P
RING = 4
CHUNK = 256
CHUNKS = D_FF // CHUNK
NIN = 20
NOUT = 8
G0 = NIN + NOUT
LOOP0 = G0 + 4
REL = SEQ + P - 1

F32 = mybir.dt.float32
F32R = mybir.dt.float32r
ALU = mybir.AluOpType
ACT = mybir.ActivationFunctionType

GROUP_COL = [3 * HALF + HALF, 3 * HALF, 0, HALF, 2 * HALF]
OUT_AT = [(2 * P * r, HALF * n) for r0 in (2, 0) for n in (0, 1) for r in (r0, r0 + 1)]
P_AT = [0, P, 3 * P, 6 * P]
P_ALL = 10 * P
PT_AT = [0, 512, 896, 1152]
PT_Q0 = [0, 128, 256, 256]
PT_ALL = 1408


def bucket_runs():
    dist = np.arange(SEQ)
    exact = BUCKETS // 2
    nf = np.maximum(dist, exact).astype(np.float32)
    large = exact + (np.log(nf / exact) / np.float32(np.log(MAX_DISTANCE / exact)) * (BUCKETS - exact)).astype(np.int32)
    bucket = np.where(dist < exact, dist, np.minimum(large, BUCKETS - 1))
    return [(int(b), int(dist[bucket == b].min()), int(dist[bucket == b].max())) for b in np.unique(bucket)]


def hybrid_layer(nc, x, rel_bias, norm_mix, w_in, gmlp_ln_g, gmlp_ln_b, w_spatial, b_spatial, out_norm_b,
                 out_norm_a, w_out, norm_ffn, w_gate, w_up, w_down, norm_final, out):
    with ExitStack() as ctx:
        def sb(name, shape, dt=F32):
            return ctx.enter_context(nc.sbuf_tensor(name, shape, dt))

        def sem(name):
            return ctx.enter_context(nc.semaphore(name))

        ps = ctx.enter_context(nc.psum_tensor("ps", [P, 8, HALF], F32))
        rel_dram = nc.dram_tensor("rel_by_distance", (HEADS, REL), F32, kind="Internal")

        xres = sb("xres", [P, TT, D])
        h_hi = sb("h_hi", [P, KT, SEQ], F32R)
        h_lo = sb("h_lo", [P, KT, SEQ], F32R)
        w_raw = sb("w_raw", [P, RING, 1024])
        w_hi = sb("w_hi", [P, RING, 1024], F32R)
        w_lo = sb("w_lo", [P, RING, 1024], F32R)
        gain = sb("gain", [P, D])
        q_hi = sb("q_hi", [P, 4, SEQ], F32R)
        q_lo = sb("q_lo", [P, 4, SEQ], F32R)
        k_hi = sb("k_hi", [P, 4, SEQ], F32R)
        k_lo = sb("k_lo", [P, 4, SEQ], F32R)
        v_hi = sb("v_hi", [P, TT, HALF], F32R)
        v_lo = sb("v_lo", [P, TT, HALF], F32R)
        ya_hi = sb("ya_hi", [P, 4, SEQ], F32R)
        ya_lo = sb("ya_lo", [P, 4, SEQ], F32R)
        yb_hi = sb("yb_hi", [P, 4, SEQ], F32R)
        yb_lo = sb("yb_lo", [P, 4, SEQ], F32R)
        bias = sb("bias", [P, HEADS, SEQ])
        work = sb("work", [P, 2 * P_ALL])
        ident = sb("ident", [P, P])
        ones = sb("ones", [P, 2])
        small = sb("small", [P, 160])

        flat = bias[:, :, :].rearrange("p h s -> p (h s)")
        u_act = flat[:, 0:2048].rearrange("p (t c) -> p t c", t=TT)
        z_act = flat[:, 2048:4096].rearrange("p (t c) -> p t c", t=TT)
        wsp_raw = flat[:, 0:1024].rearrange("p (g s) -> p g s", g=GROUPS)
        rel_row = flat[0:HEADS, 3072:3072 + REL]
        rel_tab = flat[0:HEADS, 3072 + REL:3072 + REL + BUCKETS]
        hn = work[:, 0:2 * D].rearrange("p (b d) -> p b d", b=2)
        ln_g = work[:, 0:HALF]
        ln_b = work[:, HALF:2 * HALF]
        norm_a = work[:, 2 * HALF:3 * HALF]
        prob = work[:, :].rearrange("p (b n) -> p b n", b=2)
        silu = work[:, 0:2 * HALF].rearrange("p (f n) -> p f n", f=2)
        prod = work[:, 2 * HALF:4 * HALF].rearrange("p (f n) -> p f n", f=2)
        zn_hi, zn_lo = v_hi, v_lo
        wt_hi = ya_hi[:, 0:2, :].rearrange("p a (g t) -> p (a g) t", t=P)
        wt_lo = ya_lo[:, 0:2, :].rearrange("p a (g t) -> p (a g) t", t=P)
        pt_hi = h_hi[:, :, :].rearrange("p k s -> p (k s)")
        pt_lo = h_lo[:, :, :].rearrange("p k s -> p (k s)")
        sq_new = gain[:, 0:HALF]
        sq_sum = gain[:, HALF:2 * HALF]
        act_hi, act_lo = q_hi, q_lo

        ss_x = small[:, 0:4]
        ms_x = small[:, 4:8]
        rs_x = small[:, 8:12]
        ss_a, ms_a, rs_a = small[:, 12:16], small[:, 16:20], small[:, 20:24]
        ms_b, rs_b = small[:, 24:28], small[:, 28:32]
        ms_z, rs_z = small[:, 32:36], small[:, 36:40]
        mv_z = small[:, 40:48].rearrange("p (t c) -> p t c", c=2)
        st_z = small[:, 48:72].rearrange("p (t c) -> p t c", c=6)
        half = small[:, 72:76]
        top = small[:, 76:84].rearrange("p (b t) -> p b t", b=2)
        neg_top = small[:, 84:92].rearrange("p (b t) -> p b t", b=2)
        total = small[:, 92:100].rearrange("p (b t) -> p b t", b=2)
        inv = small[:, 100:108].rearrange("p (b t) -> p b t", b=2)
        b_sp = small[:, 108:116]
        norm_b = small[:, 116:120]
        ss_2, ms_2, rs_2 = small[:, 120:124], small[:, 124:128], small[:, 128:132]
        ss_3, ms_3, rs_3 = small[:, 132:136], small[:, 136:140], small[:, 140:144]

        x_landed = [sem(f"x_landed{t}") for t in range(TT)]
        w_landed = [sem(f"w_landed{s}") for s in range(RING)]
        mix_landed = sem("mix_landed")
        ffn_landed = sem("ffn_landed")
        final_landed = sem("final_landed")
        rel_landed = sem("rel_landed")
        bsp_landed = sem("bsp_landed")
        nb_landed = sem("nb_landed")
        wsp_landed = sem("wsp_landed")
        lng_landed = sem("lng_landed")
        lnb_landed = sem("lnb_landed")
        na_landed = sem("na_landed")
        rel_stored = sem("rel_stored")
        bias_landed = [sem(f"bias_landed{f}") for f in range(HEADS // 2)]
        out_landed = sem("out_landed")

        w_hi_ready = sem("w_hi_ready")
        w_lo_ready = sem("w_lo_ready")
        w_used = sem("w_used")
        const_step = sem("const_step")
        const_ready = sem("const_ready")
        rel_ready = sem("rel_ready")
        wsp_masked = sem("wsp_masked")
        ss_ready = sem("ss_ready")
        ms_ready = sem("ms_ready")
        rs_ready = sem("rs_ready")
        hn_ready = sem("hn_ready")
        hn_turned = sem("hn_turned")
        h_hi_ready = sem("h_hi_ready")
        h_lo_ready = sem("h_lo_ready")
        proj_done = sem("proj_done")
        wsp_turned = sem("wsp_turned")
        wt_hi_ready = sem("wt_hi_ready")
        wt_lo_ready = sem("wt_lo_ready")
        z_gelu = sem("z_gelu")
        u_gelu = sem("u_gelu")
        z_stats = sem("z_stats")
        z_var = sem("z_var")
        z_ms = sem("z_ms")
        z_rs = sem("z_rs")
        z_step = sem("z_step")
        zn_hi_ready = sem("zn_hi_ready")
        zn_lo_ready = sem("zn_lo_ready")
        q_hi_ready = sem("q_hi_ready")
        q_lo_ready = sem("q_lo_ready")
        k_hi_ready = sem("k_hi_ready")
        k_lo_ready = sem("k_lo_ready")
        v_hi_ready = sem("v_hi_ready")
        v_lo_ready = sem("v_lo_ready")
        mixed = sem("mixed")
        ya_raw = sem("ya_raw")
        ya_ss = sem("ya_ss")
        ya_ms = sem("ya_ms")
        ya_rs = sem("ya_rs")
        ya_scaled = sem("ya_scaled")
        ya_turned = sem("ya_turned")
        ya_hi_ready = sem("ya_hi_ready")
        ya_lo_ready = sem("ya_lo_ready")
        pt_zeroed = sem("pt_zeroed")
        scores_done = sem("scores_done")
        logits_ready = sem("logits_ready")
        top_ready = sem("top_ready")
        exp_done = sem("exp_done")
        inv_ready = sem("inv_ready")
        p_ready = sem("p_ready")
        p_turned = sem("p_turned")
        pt_hi_ready = sem("pt_hi_ready")
        pt_lo_ready = sem("pt_lo_ready")
        pv_done = sem("pv_done")
        yb_hi_ready = sem("yb_hi_ready")
        yb_sq = sem("yb_sq")
        yb_sq_added = sem("yb_sq_added")
        yb_lo_ready = sem("yb_lo_ready")
        yb_ss = sem("yb_ss")
        yb_ms = sem("yb_ms")
        yb_rs = sem("yb_rs")
        tile_done = sem("tile_done")
        x_added = sem("x_added")
        gu_done = sem("gu_done")
        silu_ready = sem("silu_ready")
        prod_ready = sem("prod_ready")
        a_hi_ready = sem("a_hi_ready")
        a_lo_ready = sem("a_lo_ready")
        fin_ready = sem("fin_ready")

        block = ctx.enter_context(nc.Block())

        def row(v):
            return v.partition_broadcast(P)

        def w_unit(buf, i):
            return buf[:, i % RING, :]

        def pair(buf, i):
            return w_unit(buf, i).rearrange("p (k n) -> p k n", k=2)

        def quad(buf, i):
            return w_unit(buf, i).rearrange("p (k n) -> p k n", k=4)

        def rows_of(w, r, n, k):
            return w[r:r + k * P, n].rearrange("(k p) n -> p k n", p=P)

        def unit_wait(it, j):
            return it * 12 + (LOOP0 + j + 1)

        @block.sync
        def _(sp):
            def load(i, src, dst=None):
                if i >= RING:
                    sp.wait_ge(w_lo_ready, i - RING + 1)
                sp.dma_start(pair(w_raw, i) if dst is None else dst, src).then_inc(w_landed[i % RING], 16)

            def load_in(i):
                n = GROUP_COL[i // 4]
                load(i, rows_of(w_in, (i % 4) * 2 * P, slice(n, n + HALF), 2))

            sp.dma_start(xres[:, 0, :], x[0:P, :]).then_inc(x_landed[0], 16)
            sp.dma_start(xres[:, 1, :], x[P:2 * P, :]).then_inc(x_landed[1], 16)
            load_in(0)
            sp.dma_start(xres[:, 2, :], x[2 * P:3 * P, :]).then_inc(x_landed[2], 16)
            sp.dma_start(xres[:, 3, :], x[3 * P:4 * P, :]).then_inc(x_landed[3], 16)
            for i in range(1, RING):
                load_in(i)
            sp.dma_start(wsp_raw, w_spatial.rearrange("g t s -> t g s")).then_inc(wsp_landed, 16)
            for i in range(RING, NIN):
                load_in(i)
            for i in range(NOUT):
                r, n = OUT_AT[i]
                load(NIN + i, rows_of(w_out, r, slice(n, n + HALF), 2))

            for j in range(2):
                load(G0 + j, rows_of(w_gate, j * 4 * P, slice(0, CHUNK), 4), quad(w_raw, G0 + j))
            for j in range(2):
                load(G0 + 2 + j, rows_of(w_up, j * 4 * P, slice(0, CHUNK), 4), quad(w_raw, G0 + 2 + j))

            with sp.Fori(0, (CHUNKS - 1) // 2) as it:
                for cc in range(2):
                    cols = bass.ds((it * 2 + 1 + cc) * CHUNK, CHUNK)
                    for j in range(6):
                        i = 6 * cc + j
                        sp.wait_ge(w_lo_ready, unit_wait(it, i - RING))
                        if j < 4:
                            w = w_gate if j < 2 else w_up
                            sp.dma_start(quad(w_raw, LOOP0 + i), rows_of(w, (j % 2) * 4 * P, cols, 4))\
                              .then_inc(w_landed[(LOOP0 + i) % RING], 16)
                        else:
                            r = (it * 2 + cc) * CHUNK + (j - 4) * P
                            sp.dma_start(w_unit(w_raw, LOOP0 + i), w_down[bass.ds(r, P), :])\
                              .then_inc(w_landed[(LOOP0 + i) % RING], 16)
            last = LOOP0 + 6 * (CHUNKS - 1)
            for j in range(2):
                r = (CHUNKS - 1) * CHUNK + j * P
                load(last + j, w_down[r:r + P, :], w_unit(w_raw, last + j))
            for t in range(TT):
                sp.wait_ge(fin_ready, t + 1)
                sp.dma_start(out[t * P:(t + 1) * P, :], xres[:, t, :]).then_inc(out_landed, 16)
            sp.wait_ge(out_landed, 16 * TT)

        @block.gpsimd
        def _(pool):
            pool.memset(ident[:, :], 0.0).then_inc(const_step, 1)
            pool.memset(half, -0.5).then_inc(const_step, 1)
            pool.memset(ones[:, :], 1.0).then_inc(const_step, 1)
            pool.wait_ge(const_step, 3)
            pool.affine_select(out=ident[:, :], in_=ident[:, :], compare_op=ALU.not_equal, fill=1.0, base=0,
                               pattern=[[-1, P]], channel_multiplier=1).then_inc(const_ready, 1)

            def power(ss, ms, rs, ready, n, ms_sem, rs_sem, at, width):
                pool.wait_ge(ready, n)
                pool.tensor_scalar(ms, ss, 1.0 / width, EPS, ALU.mult, ALU.add).then_inc(ms_sem, 1)
                pool.wait_ge(ms_sem, at)
                pool.tensor_tensor(rs, ms, half[:, 0:rs.shape[1]], ALU.pow).then_inc(rs_sem, 1)

            for t in range(TT):
                power(ss_x[:, t:t + 1], ms_x[:, t:t + 1], rs_x[:, t:t + 1], ss_ready, t + 1, ms_ready, rs_ready,
                      t + 1, D)

            pool.wait_ge(wsp_landed, 16)
            pool.affine_select(out=wsp_raw, in_=wsp_raw, compare_op=ALU.is_ge, fill=0.0, base=0,
                               pattern=[[0, GROUPS], [-1, P]], channel_multiplier=1).then_inc(wsp_masked, 1)

            pool.wait_ge(hn_turned, TT)
            pool.dma_start(ln_g, row(gmlp_ln_g)).then_inc(lng_landed, 16)
            pool.dma_start(ln_b, row(gmlp_ln_b)).then_inc(lnb_landed, 16)
            pool.dma_start(norm_a, row(out_norm_a)).then_inc(na_landed, 16)

            pool.wait_ge(rel_landed, 16)
            pool.memset(rel_row[:, 0:P - 1], NEG)
            for b, first, final in bucket_runs():
                n = final - first + 1
                step = pool.tensor_copy(rel_row[:, P - 1 + first:P + final],
                                        rel_tab[:, b:b + 1].to_broadcast([HEADS, n]))
            step.then_inc(rel_ready, 1)
            pool.wait_ge(rel_ready, 1)
            pool.dma_start(rel_dram.ap(), rel_row).then_inc(rel_stored, 16)

            for t in range(TT):
                pool.wait_ge(z_var, t + 1)
                pool.tensor_scalar(ms_z[:, t:t + 1], mv_z[:, t, 1:2], EPS, None, ALU.add).then_inc(z_ms, 1)
                pool.wait_ge(z_ms, t + 1)
                pool.tensor_tensor(rs_z[:, t:t + 1], ms_z[:, t:t + 1], half[:, 0:1], ALU.pow).then_inc(z_rs, 1)
            power(ss_a, ms_a, rs_a, ya_ss, TT, ya_ms, ya_rs, 1, HALF)

            pool.wait_ge(ya_turned, 4)
            pool.wait_ge(rel_stored, 16)
            for f in range(HEADS // 2):
                src = bass.AP(rel_dram, 2 * f * REL, [[1, P], [REL, 2], [1, SEQ]])
                pool.dma_start(bias[:, 2 * f:2 * f + 2, :], src).then_inc(bias_landed[f], 16)

            for f in range(1, 4):
                pool.wait_ge(yb_sq, 2 * f + 2)
                if f > 1:
                    pool.wait_ge(yb_sq_added, f - 1)
                pool.tensor_tensor(sq_sum, sq_sum, sq_new, ALU.add).then_inc(yb_sq_added, 1)
            pool.wait_ge(yb_ms, 1)
            pool.tensor_tensor(rs_b, ms_b, half, ALU.pow).then_inc(yb_rs, 1)
            pool.wait_ge(yb_ss, 1)
            pool.dma_start(gain[:, :], row(norm_ffn)).then_inc(ffn_landed, 16)
            for t in range(TT):
                power(ss_2[:, t:t + 1], ms_2[:, t:t + 1], rs_2[:, t:t + 1], ss_ready, TT + t + 1, ms_ready,
                      rs_ready, TT + t + 1, D)
            pool.wait_ge(hn_ready, 2 * TT)
            pool.dma_start(gain[:, :], row(norm_final)).then_inc(final_landed, 16)
            for t in range(TT):
                power(ss_3[:, t:t + 1], ms_3[:, t:t + 1], rs_3[:, t:t + 1], ss_ready, 2 * TT + t + 1, ms_ready,
                      rs_ready, 2 * TT + t + 1, D)

        @block.scalar
        def _(act):
            act.dma_start(gain[:, :], row(norm_mix)).then_inc(mix_landed, 16)
            act.dma_start(rel_tab, rel_bias.rearrange("b h -> h b"),
                          allow_slow_non_contiguous=True).then_inc(rel_landed, 16)
            act.dma_start(b_sp, b_spatial.rearrange("g t -> t g"), allow_slow_non_contiguous=True).then_inc(bsp_landed, 16)
            act.dma_start(norm_b, out_norm_b.rearrange("(f p) -> p f", p=P),
                          allow_slow_non_contiguous=True).then_inc(nb_landed, 16)

            def split_hi(i):
                act.wait_ge(w_landed[i % RING], 16 * (i // RING + 1))
                if i >= RING:
                    act.wait_ge(w_used, i - RING + 1)
                act.activation(w_unit(w_hi, i), w_unit(w_raw, i), ACT.Copy).then_inc(w_hi_ready, 1)

            def square_x(t):
                act.wait_ge(x_landed[t], 16)
                act.activation(ps[:, 2 * t:2 * t + 2, :], xres[:, t, :].rearrange("p (b n) -> p b n", b=2),
                               ACT.Square, accum_out=ss_x[:, t:t + 1]).then_inc(ss_ready, 1)

            def h_evac(t, n, bank):
                act.wait_ge(hn_turned, n)
                act.activation(h_hi[:, :, t * P:(t + 1) * P],
                               ps[:, bank:bank + 2, :].rearrange("p b (k s) -> p (b k) s", s=P),
                               ACT.Copy).then_inc(h_hi_ready, 1)

            square_x(0)
            square_x(1)
            split_hi(0)
            h_evac(0, 1, 0)
            square_x(2)
            h_evac(1, 2, 2)
            square_x(3)
            split_hi(1)
            h_evac(2, 3, 4)
            split_hi(2)
            h_evac(3, 4, 6)
            split_hi(3)

            def zn_split(t):
                act.wait_ge(z_step, 2 * t + 2)
                act.activation(zn_hi[:, t, :], z_act[:, t, :], ACT.Copy).then_inc(zn_hi_ready, 1)

            for e in range(1, NIN):
                split_hi(e + RING - 1)
                if e == 3:
                    act.wait_ge(wsp_turned, 1)
                    act.activation(wt_hi, ps[:, 4:6, :].rearrange("p b (g s) -> p (b g) s", s=P),
                                   ACT.Copy).then_inc(wt_hi_ready, 1)
                if 4 <= e < 8:
                    t = e - 4
                    if t == 0:
                        act.wait_ge(rel_stored, 16)
                    act.wait_ge(proj_done, t + 1)
                    act.activation(z_act[:, t, :], ps[:, t, :], ACT.Gelu_apprx_tanh).then_inc(z_gelu, 1)
                    if t > 0:
                        zn_split(t - 1)
                if 8 <= e < 12:
                    t = e - 8
                    if t == 0:
                        zn_split(3)
                    act.wait_ge(proj_done, 4 + t + 1)
                    act.activation(u_act[:, t, :], ps[:, 4 + t, :], ACT.Gelu_apprx_tanh).then_inc(u_gelu, 1)
                if 12 <= e < 16:
                    f = e - 12
                    act.wait_ge(proj_done, 8 + f + 1)
                    act.activation(q_hi[:, f, :], ps[:, f, :], ACT.Copy, scale=HD ** -0.5).then_inc(q_hi_ready, 1)
                if e == 16:
                    for f in range(4):
                        act.wait_ge(proj_done, 12 + f + 1)
                        act.activation(k_hi[:, f, :], ps[:, 4 + f, :], ACT.Copy).then_inc(k_hi_ready, 1)
                if e == 17:
                    act.wait_ge(ya_raw, GROUPS)
                    for c in range(TT):
                        act.activation(u_act[:, c, :], z_act[:, c, :], ACT.Square,
                                       accum_out=ss_a[:, c:c + 1]).then_inc(ya_ss, 1)
                if e == 19:
                    for f in range(4):
                        act.wait_ge(ya_turned, f + 1)
                        act.activation(ya_hi[:, f, :], ps[:, 4 + f, :], ACT.Copy).then_inc(ya_hi_ready, 1)
            for t in range(TT):
                act.wait_ge(proj_done, 16 + t + 1)
                act.activation(v_hi[:, t, :], ps[:, t, :], ACT.Copy).then_inc(v_hi_ready, 1)

            def turned_hi(h, kt):
                b = h % 2
                act.wait_ge(p_turned, 4 * h + kt + 1)
                if h >= 2:
                    act.wait_ge(pv_done, h - 1)
                elif h == 0 and kt == 0:
                    act.wait_ge(pt_zeroed, 4)
                n = (TT - kt) * P
                at = b * PT_ALL + PT_AT[kt] + kt * P - PT_Q0[kt]
                act.activation(pt_hi[:, at:at + n], ps[:, kt % 2, kt * P:SEQ], ACT.Copy).then_inc(pt_hi_ready, 1)

            def yb_evac(h):
                r, f = (h % 2) * HD, h // 2
                act.wait_ge(pv_done, h + 1)
                if h == 0:
                    act.wait_ge(nb_landed, 16)
                act.activation(yb_hi[r:r + HD, f, :], ps[r:r + HD, 2, :], ACT.Copy,
                               scale=norm_b[r:r + HD, f:f + 1]).then_inc(yb_hi_ready, 1)
                if f > 1:
                    act.wait_ge(yb_sq_added, f - 1)
                dst = sq_new if f else sq_sum
                act.activation(dst[r:r + HD, :], ps[r:r + HD, 2, :], ACT.Square).then_inc(yb_sq, 1)

            for s in range(HEADS + 2):
                if 0 <= s - 1 < HEADS:
                    turned_hi(s - 1, 0)
                    turned_hi(s - 1, 1)
                if s < HEADS:
                    b = s % 2
                    act.wait_ge(top_ready, s + 1)
                    for t in range(TT):
                        p_t = prob[:, b, P_AT[t]:P_AT[t] + (t + 1) * P]
                        act.activation(p_t, p_t, ACT.Exp, bias=neg_top[:, b, t:t + 1],
                                       accum_out=total[:, b, t:t + 1]).then_inc(exp_done, 1)
                if 0 <= s - 1 < HEADS:
                    turned_hi(s - 1, 2)
                    turned_hi(s - 1, 3)
                if s == 4:
                    split_hi(23)
                if s == 6:
                    split_hi(24)
                    split_hi(25)
                if s >= 2:
                    yb_evac(s - 2)
            split_hi(26)
            split_hi(27)

            def square_rows(t, n, added, ss):
                act.wait_ge(x_added, added)
                if t >= 2 and n < 2 * TT:
                    act.wait_ge(hn_turned, n - 1)
                elif t >= 2:
                    act.wait_ge(ss_ready, n - 1)
                act.activation(hn[:, t % 2, :], xres[:, t, :], ACT.Square,
                               accum_out=ss[:, t:t + 1]).then_inc(ss_ready, 1)

            split_hi(G0)
            split_hi(G0 + 1)
            for t in range(TT):
                if t >= 2:
                    h_evac(t - 2, TT + t - 1, 2 * (t % 2))
                square_rows(t, TT + t, 8 + 4 + t + 1, ss_2)
            h_evac(2, TT + 3, 0)
            h_evac(3, TT + 4, 2)

            def ffn(c, it, cc):
                def split_c(j):
                    i = LOOP0 + 6 * cc + j
                    if it is None:
                        split_hi(i)
                        return
                    act.wait_ge(w_landed[i % RING], (it * 3 + (i // RING + 1)) * 16)
                    act.wait_ge(w_used, unit_wait(it, 6 * cc + j - RING))
                    act.activation(w_unit(w_hi, i), w_unit(w_raw, i), ACT.Copy).then_inc(w_hi_ready, 1)

                par = (1 + cc) % 2
                bank = 4 if it is None else 0
                split_c(2 if it is not None else 4)
                split_c(3 if it is not None else 5)
                for f in range(2):
                    act.wait_ge(gu_done, c * 4 + (f + 1))
                    act.activation(silu[:, f, :], ps[:, bank + f, :], ACT.Silu).then_inc(silu_ready, 1)
                if it is not None:
                    split_c(4)
                    split_c(5)
                for f in range(2):
                    act.wait_ge(prod_ready, c * 2 + (f + 1))
                    if it is not None:
                        act.wait_ge(tile_done, (c - 1) * 8 + 16)
                    act.activation(act_hi[:, 2 * par + f, :], prod[:, f, :], ACT.Copy).then_inc(a_hi_ready, 1)
                split_c(6)
                split_c(7)

            ffn(0, None, -1)
            with act.Fori(0, (CHUNKS - 1) // 2) as it:
                for cc in range(2):
                    ffn(it * 2 + (1 + cc), it, cc)
            for t in range(TT):
                square_rows(t, 2 * TT + t, 16 + 8 * (CHUNKS - 1) + 2 * t + 2, ss_3)

        @block.vector
        def _(dve):
            def split_lo(i):
                dve.wait_ge(w_hi_ready, i + 1)
                dve.tensor_tensor(w_unit(w_lo, i), w_unit(w_raw, i), w_unit(w_hi, i).bitcast(F32),
                                  ALU.subtract).then_inc(w_lo_ready, 1)

            def norm_rows(t, n, rs, dst):
                dve.wait_ge(rs_ready, n + 1)
                dve.scalar_tensor_tensor(out=dst, in0=xres[:, t, :], scalar=rs[:, t:t + 1], in1=gain[:, :],
                                         op0=ALU.mult, op1=ALU.mult)\
                   .then_inc(hn_ready if n < 2 * TT else fin_ready, 1)

            def h_evac(t, n, bank):
                dve.wait_ge(h_hi_ready, n)
                dve.tensor_tensor(h_lo[:, :, t * P:(t + 1) * P],
                                  ps[:, bank:bank + 2, :].rearrange("p b (k s) -> p (b k) s", s=P),
                                  h_hi[:, :, t * P:(t + 1) * P].bitcast(F32), ALU.subtract)\
                   .then_inc(h_lo_ready, 1)

            dve.wait_ge(mix_landed, 16)
            norm_rows(0, 0, rs_x, hn[:, 0, :])
            norm_rows(1, 1, rs_x, hn[:, 1, :])
            split_lo(0)
            h_evac(0, 1, 0)
            dve.wait_ge(hn_turned, 1)
            norm_rows(2, 2, rs_x, hn[:, 0, :])
            h_evac(1, 2, 2)
            dve.wait_ge(hn_turned, 2)
            norm_rows(3, 3, rs_x, hn[:, 1, :])
            split_lo(1)
            h_evac(2, 3, 4)
            split_lo(2)
            h_evac(3, 4, 6)
            split_lo(3)

            def zn_split(t):
                dve.wait_ge(zn_hi_ready, t + 1)
                dve.tensor_tensor(zn_lo[:, t, :], z_act[:, t, :], zn_hi[:, t, :].bitcast(F32),
                                  ALU.subtract).then_inc(zn_lo_ready, 1)

            def layer_norm(t):
                dve.wait_ge(z_gelu, t + 1)
                dve.bn_stats(st_z[:, t, :], z_act[:, t, :]).then_inc(z_stats, 1)
                dve.wait_ge(z_stats, t + 1)
                dve.bn_aggr(mv_z[:, t, :], st_z[:, t, :]).then_inc(z_var, 1)
                if t == 0:
                    dve.wait_ge(lng_landed, 16)
                    dve.wait_ge(lnb_landed, 16)
                dve.wait_ge(z_rs, t + 1)
                dve.scalar_tensor_tensor(out=z_act[:, t, :], in0=z_act[:, t, :], scalar=mv_z[:, t, 0:1], in1=ln_g,
                                         op0=ALU.subtract, op1=ALU.mult).then_inc(z_step, 1)
                dve.wait_ge(z_step, 2 * t + 1)
                dve.scalar_tensor_tensor(out=z_act[:, t, :], in0=z_act[:, t, :], scalar=rs_z[:, t:t + 1], in1=ln_b,
                                         op0=ALU.mult, op1=ALU.add).then_inc(z_step, 1)

            for e in range(1, NIN):
                split_lo(e + RING - 1)
                if e == 3:
                    dve.wait_ge(wt_hi_ready, 1)
                    dve.tensor_tensor(wt_lo, ps[:, 4:6, :].rearrange("p b (g s) -> p (b g) s", s=P),
                                      wt_hi.bitcast(F32), ALU.subtract).then_inc(wt_lo_ready, 1)
                if 4 <= e < 8:
                    layer_norm(e - 4)
                    if e > 4:
                        zn_split(e - 5)
                if e == 8:
                    zn_split(3)
                if 12 <= e < 16:
                    f = e - 12
                    dve.wait_ge(q_hi_ready, f + 1)
                    dve.scalar_tensor_tensor(out=q_lo[:, f, :], in0=ps[:, f, :], scalar=HD ** -0.5,
                                             in1=q_hi[:, f, :].bitcast(F32), op0=ALU.mult, op1=ALU.subtract)\
                       .then_inc(q_lo_ready, 1)
                if e == 16:
                    for f in range(4):
                        dve.wait_ge(k_hi_ready, f + 1)
                        dve.tensor_tensor(k_lo[:, f, :], ps[:, 4 + f, :], k_hi[:, f, :].bitcast(F32),
                                          ALU.subtract).then_inc(k_lo_ready, 1)
                if e == 17:
                    dve.wait_ge(bsp_landed, 16)
                    dve.wait_ge(u_gelu, TT)
                    for g in range(GROUPS):
                        dve.wait_ge(mixed, g // 2 + 1)
                        at = slice(g * GD, (g + 1) * GD)
                        dve.scalar_tensor_tensor(
                            out=z_act[:, :, at],
                            in0=ps[:, 4 + g // 2, (g % 2) * 256:(g % 2 + 1) * 256].rearrange("p (c d) -> p c d", d=GD),
                            scalar=b_sp[:, g:g + 1], in1=u_act[:, :, at], op0=ALU.add, op1=ALU.mult)\
                           .then_inc(ya_raw, 1)
                if e == 18:
                    dve.wait_ge(na_landed, 16)
                    dve.wait_ge(ya_rs, 1)
                    for c in range(TT):
                        dve.scalar_tensor_tensor(out=z_act[:, c, :], in0=z_act[:, c, :], scalar=rs_a[:, c:c + 1],
                                                 in1=norm_a, op0=ALU.mult, op1=ALU.mult).then_inc(ya_scaled, 1)
                if e == 19:
                    for f in range(4):
                        dve.wait_ge(ya_hi_ready, f + 1)
                        dve.tensor_tensor(ya_lo[:, f, :], ps[:, 4 + f, :], ya_hi[:, f, :].bitcast(F32),
                                          ALU.subtract).then_inc(ya_lo_ready, 1)
            for t in range(TT):
                dve.wait_ge(v_hi_ready, t + 1)
                dve.tensor_tensor(v_lo[:, t, :], ps[:, t, :], v_hi[:, t, :].bitcast(F32),
                                  ALU.subtract).then_inc(v_lo_ready, 1)
            for b in range(2):
                for buf in (pt_hi, pt_lo):
                    at = b * PT_ALL + PT_AT[3]
                    dve.memset(buf[:, at:at + P].bitcast(F32), 0.0).then_inc(pt_zeroed, 1)

            def add_tile(j):
                n, t = j % 8 // 4, j % 4
                dve.wait_ge(tile_done, j + 1)
                dst = xres[:, t, n * HALF:(n + 1) * HALF]
                if j < 8:
                    dve.tensor_tensor(dst, ps[:, 3, :], dst, ALU.add).then_inc(x_added, 1)
                else:
                    if j == 8:
                        dve.wait_ge(yb_rs, 1)
                    dve.wait_ge(x_added, j - 7)
                    dve.scalar_tensor_tensor(out=dst, in0=ps[:, 4 + j % 4, :], scalar=rs_b[:, t:t + 1], in1=dst,
                                             op0=ALU.mult, op1=ALU.add).then_inc(x_added, 1)

            def turned_lo(h, kt):
                n = (TT - kt) * P
                at = (h % 2) * PT_ALL + PT_AT[kt] + kt * P - PT_Q0[kt]
                dve.wait_ge(pt_hi_ready, 4 * h + kt + 1)
                dve.tensor_tensor(pt_lo[:, at:at + n], ps[:, kt % 2, kt * P:SEQ], pt_hi[:, at:at + n].bitcast(F32),
                                  ALU.subtract).then_inc(pt_lo_ready, 1)

            for s in range(HEADS + 2):
                if s < HEADS:
                    b = s % 2
                    dve.wait_ge(bias_landed[s // 2], 16)
                    if s >= 2:
                        dve.wait_ge(p_turned, 4 * (s - 1))
                    for t in range(TT):
                        n = (t + 1) * P
                        dve.wait_ge(scores_done, 4 * s + t + 1)
                        dve.tensor_tensor_reduce(out=prob[:, b, P_AT[t]:P_AT[t] + n], in0=ps[:, 4 + t, 0:n],
                                                 in1=bias[:, s, 0:n][:, ::-1], scale=1.0, scalar=-3e38,
                                                 op0=ALU.add, op1=ALU.max, accum_out=top[:, b, t:t + 1])\
                           .then_inc(logits_ready, 1)
                    dve.wait_ge(logits_ready, 4 * s + 4)
                    dve.tensor_scalar(neg_top[:, b, :], top[:, b, :], -1.0, None, ALU.mult).then_inc(top_ready, 1)
                if 0 <= s - 1 < HEADS:
                    turned_lo(s - 1, 0)
                    turned_lo(s - 1, 1)
                    add_tile(s - 1)
                    turned_lo(s - 1, 2)
                    turned_lo(s - 1, 3)
                if s < HEADS:
                    b = s % 2
                    dve.wait_ge(exp_done, 4 * s + 4)
                    dve.reciprocal(inv[:, b, :], total[:, b, :]).then_inc(inv_ready, 1)
                    dve.wait_ge(inv_ready, s + 1)
                    for t in range(TT):
                        p_t = prob[:, b, P_AT[t]:P_AT[t] + (t + 1) * P]
                        dve.tensor_scalar(p_t, p_t, inv[:, b, t:t + 1], None, ALU.mult).then_inc(p_ready, 1)
                if s == 4:
                    split_lo(23)
                if s == 6:
                    split_lo(24)
                    split_lo(25)
                if s >= 2:
                    h, r, f = s - 2, (s % 2) * HD, (s - 2) // 2
                    dve.wait_ge(yb_sq, h + 1)
                    dve.scalar_tensor_tensor(out=yb_lo[r:r + HD, f, :], in0=ps[r:r + HD, 2, :],
                                             scalar=norm_b[r:r + HD, f:f + 1],
                                             in1=yb_hi[r:r + HD, f, :].bitcast(F32),
                                             op0=ALU.mult, op1=ALU.subtract).then_inc(yb_lo_ready, 1)
            split_lo(26)
            split_lo(27)
            dve.wait_ge(yb_ss, 1)
            dve.tensor_scalar(ms_b, ps[:, 0, 0:TT], 1.0 / HALF, EPS, ALU.mult, ALU.add).then_inc(yb_ms, 1)
            for j in range(8, 12):
                add_tile(j)
            split_lo(G0)
            split_lo(G0 + 1)
            dve.wait_ge(ffn_landed, 16)
            add_tile(12)
            for t in range(TT):
                if t + 1 < TT:
                    add_tile(13 + t)
                if t >= 2:
                    h_evac(t - 2, TT + t - 1, 2 * (t % 2))
                norm_rows(t, TT + t, rs_2, hn[:, t % 2, :])
            h_evac(2, TT + 3, 0)
            h_evac(3, TT + 4, 2)

            def ffn(c, it, cc):
                def split_c(j):
                    i = LOOP0 + 6 * cc + j
                    if it is None:
                        split_lo(i)
                        return
                    dve.wait_ge(w_hi_ready, unit_wait(it, 6 * cc + j))
                    dve.tensor_tensor(w_unit(w_lo, i), w_unit(w_raw, i), w_unit(w_hi, i).bitcast(F32),
                                      ALU.subtract).then_inc(w_lo_ready, 1)

                par = (1 + cc) % 2
                bank = 4 if it is None else 0
                split_c(2 if it is not None else 4)
                split_c(3 if it is not None else 5)
                if it is not None:
                    split_c(4)
                    split_c(5)
                for f in range(2):
                    dve.wait_ge(gu_done, c * 4 + (3 + f))
                    dve.wait_ge(silu_ready, c * 2 + (f + 1))
                    dve.tensor_tensor(prod[:, f, :], silu[:, f, :], ps[:, bank + 2 + f, :], ALU.mult)\
                       .then_inc(prod_ready, 1)
                for f in range(2):
                    dve.wait_ge(a_hi_ready, c * 2 + (f + 1))
                    dve.tensor_tensor(act_lo[:, 2 * par + f, :], prod[:, f, :],
                                      act_hi[:, 2 * par + f, :].bitcast(F32), ALU.subtract).then_inc(a_lo_ready, 1)
                split_c(6)
                split_c(7)
                if it is not None:
                    for j in range(8):
                        add_down(c - 1, j)

            def add_down(c, j):
                t, n = j // 2, j % 2
                dst = xres[:, t, n * HALF:(n + 1) * HALF]
                dve.wait_ge(tile_done, c * 8 + (17 + j))
                dve.wait_ge(x_added, c * 8 + (9 + j))
                dve.tensor_tensor(dst, ps[:, 4 + j % 4, :], dst, ALU.add).then_inc(x_added, 1)

            ffn(0, None, -1)
            with dve.Fori(0, (CHUNKS - 1) // 2) as it:
                for cc in range(2):
                    ffn(it * 2 + (1 + cc), it, cc)
            dve.wait_ge(final_landed, 16)
            for t in range(TT):
                add_down(CHUNKS - 1, 2 * t)
                add_down(CHUNKS - 1, 2 * t + 1)
                if t > 0:
                    norm_rows(t - 1, 2 * TT + t - 1, rs_3, xres[:, t - 1, :])
            norm_rows(TT - 1, 3 * TT - 1, rs_3, xres[:, TT - 1, :])

        @block.tensor
        def _(pe):
            def mm3(dst, a, b, at, start, stop, frees=False):
                (a_hi, a_lo), (b_hi, b_lo) = a, b
                sa, sbb = at
                first = pe.matmul(dst, a_hi[sa], b_hi[sbb], start=start, stop=False)
                if frees:
                    first.then_inc(w_used, 1)
                pe.matmul(dst, a_hi[sa], b_lo[sbb], start=False, stop=False)
                return pe.matmul(dst, a_lo[sa], b_hi[sbb], start=False, stop=stop)

            H, W = (h_hi, h_lo), (w_hi, w_lo)
            everything = slice(None)

            def w2(i):
                return pair(w_hi, i), pair(w_lo, i)

            def turn_rows(t, n, bank):
                pe.wait_ge(hn_ready, n)
                for k in range(KT):
                    last = pe.transpose(ps[:, bank + k // 4, (k % 4) * P:(k % 4 + 1) * P],
                                        hn[:, t % 2, k * P:(k + 1) * P], ident[:, :])
                last.then_inc(hn_turned, 1)

            pe.wait_ge(const_ready, 1)
            for t in range(TT):
                turn_rows(t, t + 1, 2 * t)

            for i in range(NIN):
                group, j = divmod(i, 4)
                bank = 4 * (group % 2)
                if i == 4:
                    pe.wait_ge(wt_lo_ready, 1)
                if i == 8:
                    pe.wait_ge(z_gelu, 4)
                if i == 12:
                    pe.wait_ge(u_gelu, 4)
                if i == 16:
                    pe.wait_ge(q_lo_ready, 4)
                pe.wait_ge(w_lo_ready, i + 1)
                for m in range(4):
                    if i == 0:
                        pe.wait_ge(h_lo_ready, m + 1)
                    if group in (2, 3):
                        for kk in range(2):
                            last = mm3(ps[:, bank + m, :], w2(i), H,
                                       ((everything, kk, slice(m * P, (m + 1) * P)), (everything, 2 * j + kk)),
                                       j == 0 and kk == 0, j == 3 and kk == 1, i > 0 and j + m + kk == 0)
                    else:
                        for kk in range(2):
                            last = mm3(ps[:, bank + m, :], H, w2(i),
                                       ((everything, 2 * j + kk, slice(m * P, (m + 1) * P)), (everything, kk)),
                                       j == 0 and kk == 0, j == 3 and kk == 1, i > 0 and j + m + kk == 0)
                    if j == 3:
                        last.then_inc(proj_done, 1)
                if j < 3:
                    last.then_inc(w_used, 1)
                if i == 2:
                    pe.wait_ge(wsp_masked, 1)
                    for g in range(GROUPS):
                        last = pe.transpose(ps[:, 4 + g // 4, (g % 4) * P:(g % 4 + 1) * P], wsp_raw[:, g, :],
                                            ident[:, :])
                    last.then_inc(wsp_turned, 1)
                if i == 16:
                    pe.wait_ge(k_lo_ready, 4)
                    pe.wait_ge(zn_lo_ready, 4)
                    for g in range(GROUPS):
                        last = mm3(ps[:, 4 + g // 2, (g % 2) * 256:(g % 2 + 1) * 256], (wt_hi, wt_lo),
                                   (zn_hi, zn_lo),
                                   ((everything, g), (everything, everything, slice(g * GD, (g + 1) * GD))),
                                   True, True)
                        if g % 2:
                            last.then_inc(mixed, 1)
                if i == 18:
                    pe.wait_ge(ya_scaled, 4)
                    for f in range(4):
                        for c in range(TT):
                            last = pe.transpose(ps[:, 4 + f, c * P:(c + 1) * P], z_act[:, c, f * P:(f + 1) * P],
                                                ident[:, :])
                        last.then_inc(ya_turned, 1)

            def out_tile(j):
                n, t = j % 8 // 4, j % 4
                y = (ya_hi, ya_lo) if j < 8 else (yb_hi, yb_lo)
                first = NIN + 2 * (j // 4)
                bank = 3 if j < 8 else 4 + j % 4
                if 0 < j < 8:
                    pe.wait_ge(x_added, j)
                if j >= 12:
                    pe.wait_ge(x_added, j - 3)
                for k in range(4):
                    i = first + k // 2
                    pe.wait_ge(w_lo_ready, i + 1)
                    if j == 8 and k == 3:
                        pe.wait_ge(yb_lo_ready, HEADS)
                    last = mm3(ps[:, bank, :], y, w2(i),
                               ((everything, k, slice(t * P, (t + 1) * P)), (everything, k % 2)), k == 0, k == 3,
                               k == 0 and j in (4, 8, 12))
                    if k == 1 and t == 3:
                        last.then_inc(w_used, 1)
                    if k == 3:
                        last.then_inc(tile_done, 1)

            def scores(h):
                f, r = h // 2, slice((h % 2) * HD, (h % 2 + 1) * HD)
                for t in range(TT):
                    if h == 0:
                        pe.wait_ge(ya_lo_ready, t + 1)
                    else:
                        pe.wait_ge(logits_ready, 4 * (h - 1) + t + 1)
                    n = max((t + 1) * P, 256)
                    mm3(ps[:, 4 + t, 0:n], (q_hi, q_lo), (k_hi, k_lo),
                        ((r, f, slice(t * P, (t + 1) * P)), (r, f, slice(0, n))), True, True, h + t == 0)\
                        .then_inc(scores_done, 1)

            def turn_prob(h, kt):
                n = 4 * h + kt
                if n == 0:
                    pe.wait_ge(v_lo_ready, 4)
                if n >= 2:
                    pe.wait_ge(pt_lo_ready, n - 1)
                for t in range(kt, TT):
                    pe.wait_ge(p_ready, 4 * h + t + 1)
                    at = P_AT[t] + kt * P
                    last = pe.transpose(ps[:, kt % 2, t * P:(t + 1) * P], prob[:, h % 2, at:at + P], ident[:, :])
                last.then_inc(p_turned, 1)

            def values(h):
                f, b = h // 2, h % 2
                pe.wait_ge(pt_lo_ready, 4 * h + 4)
                if h == 0:
                    pe.wait_ge(pt_zeroed, 4)
                else:
                    pe.wait_ge(yb_lo_ready, h)
                for kt in range(TT):
                    at = b * PT_ALL + PT_AT[kt]
                    n = SEQ - PT_Q0[kt]
                    last = mm3(ps[:, 2, PT_Q0[kt]:SEQ], (v_hi, v_lo), (pt_hi, pt_lo),
                               ((everything, kt, slice(f * P, (f + 1) * P)), (everything, slice(at, at + n))),
                               kt == 0, kt == 3)
                last.then_inc(pv_done, 1)

            for s in range(HEADS + 2):
                if s < HEADS:
                    scores(s)
                if 0 <= s - 1 < HEADS:
                    turn_prob(s - 1, 0)
                    turn_prob(s - 1, 1)
                    out_tile(s - 1)
                    turn_prob(s - 1, 2)
                    turn_prob(s - 1, 3)
                if s >= 2:
                    values(s - 2)

            out_tile(8)
            pe.wait_ge(yb_sq_added, 3)
            for t in range(TT):
                last = pe.matmul(ps[:, 0, t:t + 1], sq_sum[:, t * P:(t + 1) * P], ones[:, 0:1],
                                 start=True, stop=True)
            last.then_inc(yb_ss, 1)
            for j in range(9, 15):
                out_tile(j)
            turn_rows(0, TT + 1, 0)
            out_tile(15)
            turn_rows(1, TT + 2, 2)

            def half_of(units, f, s, bank, frees):
                for k in range(KT):
                    i = units + k // 4
                    last = mm3(ps[:, bank, s], (quad(w_hi, i), quad(w_lo, i)), H,
                               ((everything, k % 4, slice(f * P, (f + 1) * P)), (everything, k, s)),
                               k == 0, k == KT - 1, frees and k == 0)
                    if f == 1 and k == 3 and s.stop == SEQ:
                        last.then_inc(w_used, 1)
                return last

            pe.wait_ge(h_lo_ready, TT + 2)
            for m in range(4):
                if m < 2:
                    pe.wait_ge(x_added, 13 + m)
                else:
                    pe.wait_ge(x_added, 16)
                pe.wait_ge(w_lo_ready, G0 + 2 * (m // 2) + 2)
                half_of(G0 + 2 * (m // 2), m % 2, slice(0, 256), 4 + m, m == 0)
                if m == 1:
                    pe.wait_ge(h_lo_ready, TT + 1)
                    turn_rows(2, TT + 3, 0)
                    pe.wait_ge(h_lo_ready, TT + 2)
                    turn_rows(3, TT + 4, 2)
            pe.wait_ge(h_lo_ready, TT + 4)
            for m in range(4):
                half_of(G0 + 2 * (m // 2), m % 2, slice(256, SEQ), 4 + m, m == 2).then_inc(gu_done, 1)

            def down(c, par, units, ready):
                pe.wait_ge(a_lo_ready, c * 2 + 2)
                ready()
                for j in range(8):
                    t, n = j // 2, j % 2
                    pe.wait_ge(x_added, c * 8 + (13 + j))
                    for f in range(2):
                        i = units + f
                        last = mm3(ps[:, 4 + j % 4, :], (act_hi, act_lo), (w_unit(w_hi, i), w_unit(w_lo, i)),
                                   ((everything, 2 * par + f, slice(t * P, (t + 1) * P)),
                                    (everything, slice(n * HALF, (n + 1) * HALF))), f == 0, f == 1, j + f == 0)
                        if j == 7 and f == 0:
                            last.then_inc(w_used, 1)
                    last.then_inc(tile_done, 1)

            with pe.Fori(0, (CHUNKS - 1) // 2) as it:
                for cc in range(2):
                    c = it * 2 + (1 + cc)
                    for m in range(4):
                        pe.wait_ge(w_lo_ready, unit_wait(it, 6 * cc + 2 * (m // 2) + 1))
                        pe.wait_ge(silu_ready if m < 2 else prod_ready, c * 2 - (1 - m % 2))
                        half_of(LOOP0 + 6 * cc + 2 * (m // 2), m % 2, slice(0, SEQ), m, m % 2 == 0)\
                            .then_inc(gu_done, 1)
                    down(c - 1, cc, LOOP0 + 6 * cc + 4,
                         lambda: pe.wait_ge(w_lo_ready, unit_wait(it, 6 * cc + 5)))
            last = LOOP0 + 6 * (CHUNKS - 1)
            down(CHUNKS - 1, (CHUNKS - 1) % 2, last, lambda: pe.wait_ge(w_lo_ready, last + 2))


_INS = ['x', 'rel_bias', 'norm_mix', 'w_in', 'gmlp_ln_g', 'gmlp_ln_b', 'w_spatial', 'b_spatial', 'out_norm_b',
        'out_norm_a', 'w_out', 'norm_ffn', 'w_gate', 'w_up', 'w_down', 'norm_final']


def kernel(**inputs):
    import numpy as _np
    import concourse.bacc as _bacc
    from concourse import mybir as _mybir
    from concourse.bass_utils import run_bass_kernel_spmd as _run

    nc = _bacc.Bacc("TRN2", target_bir_lowering=False, num_devices=1)
    arrays, args = {}, []
    for name in _INS:
        a = _np.ascontiguousarray(inputs[name])
        if name not in ('rel_bias', 'norm_final'):
            a = a[0]
        a = _np.ascontiguousarray(a)
        arrays[f"in_{name}_dram"] = a
        args.append(nc.dram_tensor(f"in_{name}_dram", a.shape, _mybir.dt.from_np(a.dtype), kind="ExternalInput").ap())
    args.append(nc.dram_tensor("out_dram", (SEQ, D), F32, kind="ExternalOutput").ap())
    hybrid_layer(nc, *args)
    r = _run(nc, [arrays], core_ids=[0])
    return r.results[0]["out_dram"].reshape(1, SEQ, D)
```

```python
from contextlib import ExitStack

import numpy as np

import concourse.bass as bass
from concourse import mybir

P = 128
D = 1024
SEQ = 512
HEADS = 8
HD = 64
GROUPS = 8
GD = 64
HALF = 512
D_FF = 2816
BUCKETS = 32
MAX_DISTANCE = 128
EPS = 1e-6
NEG = -1e9
TT = SEQ // P
KT = D // P
RING = 4
CHUNK = 256
CHUNKS = D_FF // CHUNK
NIN = 20
NOUT = 8
LOOP0 = NIN + NOUT
BY_POOL = 2
BANK0 = [7, 4, 5, 6]
REL = SEQ + P - 1

F32 = mybir.dt.float32
F32R = mybir.dt.float32r
ALU = mybir.AluOpType
ACT = mybir.ActivationFunctionType

GROUP_COL = [3 * HALF + HALF, 3 * HALF, 0, HALF, 2 * HALF]
OUT_AT = [(2 * P * r, HALF * n) for r0 in (2, 0) for n in (0, 1) for r in (r0, r0 + 1)]
P_AT = [0, P, 3 * P, 6 * P]
P_ALL = 10 * P
PT_AT = [0, 512, 896, 1152]
PT_Q0 = [0, 128, 256, 256]
PT_ALL = 1408


def bucket_runs():
    dist = np.arange(SEQ)
    exact = BUCKETS // 2
    nf = np.maximum(dist, exact).astype(np.float32)
    large = exact + (np.log(nf / exact) / np.float32(np.log(MAX_DISTANCE / exact)) * (BUCKETS - exact)).astype(np.int32)
    bucket = np.where(dist < exact, dist, np.minimum(large, BUCKETS - 1))
    return [(int(b), int(dist[bucket == b].min()), int(dist[bucket == b].max())) for b in np.unique(bucket)]


def hybrid_layer(nc, x, rel_bias, norm_mix, w_in, gmlp_ln_g, gmlp_ln_b, w_spatial, b_spatial, out_norm_b,
                 out_norm_a, w_out, norm_ffn, w_gate, w_up, w_down, norm_final, out):
    with ExitStack() as ctx:
        def sb(name, shape, dt=F32):
            return ctx.enter_context(nc.sbuf_tensor(name, shape, dt))

        def sem(name):
            return ctx.enter_context(nc.semaphore(name))

        ps = ctx.enter_context(nc.psum_tensor("ps", [P, 8, HALF], F32))
        rel_dram = nc.dram_tensor("rel_by_distance", (HEADS, REL), F32, kind="Internal")

        xres = sb("xres", [P, TT, D])
        h_hi = sb("h_hi", [P, KT, SEQ], F32R)
        h_lo = sb("h_lo", [P, KT, SEQ], F32R)
        w_raw = sb("w_raw", [P, RING, 1024])
        w_hi = sb("w_hi", [P, RING, 1024], F32R)
        w_lo = sb("w_lo", [P, RING, 1024], F32R)
        gain = sb("gain", [P, D])
        q_hi = sb("q_hi", [P, 4, SEQ], F32R)
        q_lo = sb("q_lo", [P, 4, SEQ], F32R)
        k_hi = sb("k_hi", [P, 4, SEQ], F32R)
        k_lo = sb("k_lo", [P, 4, SEQ], F32R)
        v_hi = sb("v_hi", [P, TT, HALF], F32R)
        v_lo = sb("v_lo", [P, TT, HALF], F32R)
        ya_hi = sb("ya_hi", [P, 4, SEQ], F32R)
        ya_lo = sb("ya_lo", [P, 4, SEQ], F32R)
        yb_hi = sb("yb_hi", [P, 4, SEQ], F32R)
        yb_lo = sb("yb_lo", [P, 4, SEQ], F32R)
        bias = sb("bias", [P, HEADS, SEQ])
        work = sb("work", [P, 2 * P_ALL])
        ident = sb("ident", [P, P])
        ones = sb("ones", [P, 2])
        small = sb("small", [P, 160])

        flat = bias[:, :, :].rearrange("p h s -> p (h s)")
        u_act = flat[:, 0:2048].rearrange("p (t c) -> p t c", t=TT)
        z_act = flat[:, 2048:4096].rearrange("p (t c) -> p t c", t=TT)
        wsp_raw = flat[:, 0:1024].rearrange("p (g s) -> p g s", g=GROUPS)
        rel_row = flat[0:HEADS, 3072:3072 + REL]
        rel_tab = flat[0:HEADS, 3072 + REL:3072 + REL + BUCKETS]
        hn = work[:, 0:2 * D].rearrange("p (b d) -> p b d", b=2)
        hn_more = flat[:, 1024:3072].rearrange("p (b d) -> p b d", b=2)
        ln_g = work[:, 0:HALF]
        ln_b = work[:, HALF:2 * HALF]
        norm_a = work[:, 2 * HALF:3 * HALF]
        prob = work[:, :].rearrange("p (b n) -> p b n", b=2)
        silu = work[:, 0:2 * HALF].rearrange("p (f n) -> p f n", f=2)
        prod = work[:, 2 * HALF:4 * HALF].rearrange("p (f n) -> p f n", f=2)
        zn_hi, zn_lo = v_hi, v_lo
        wt_hi = ya_hi[:, 0:2, :].rearrange("p a (g t) -> p (a g) t", t=P)
        wt_lo = ya_lo[:, 0:2, :].rearrange("p a (g t) -> p (a g) t", t=P)
        pt_hi = h_hi[:, :, :].rearrange("p k s -> p (k s)")
        pt_lo = h_lo[:, :, :].rearrange("p k s -> p (k s)")
        sq_new = gain[:, 0:HALF]
        sq_sum = gain[:, HALF:2 * HALF]
        act_hi, act_lo = q_hi, q_lo
        gain_ffn = flat[:, 0:D]
        last_row = flat[:, D:2 * D]
        side_raw = [flat[:, 1024 * i:1024 * (i + 1)] for i in range(4)]
        side_hi = [b[:, 2 * i:2 * i + 2, :].rearrange("p a n -> p (a n)") for b in (k_hi, ya_hi) for i in range(2)]
        side_lo = [b[:, 2 * i:2 * i + 2, :].rearrange("p a n -> p (a n)") for b in (k_lo, ya_lo) for i in range(2)]

        ss_x = small[:, 0:4]
        ms_x = small[:, 4:8]
        rs_x = small[:, 8:12]
        ss_a, ms_a, rs_a = small[:, 12:16], small[:, 16:20], small[:, 20:24]
        ms_b, rs_b = small[:, 24:28], small[:, 28:32]
        ms_z, rs_z = small[:, 32:36], small[:, 36:40]
        mv_z = small[:, 40:48].rearrange("p (t c) -> p t c", c=2)
        st_z = small[:, 48:72].rearrange("p (t c) -> p t c", c=6)
        half = small[:, 72:76]
        top = small[:, 76:84].rearrange("p (b t) -> p b t", b=2)
        neg_top = small[:, 84:92].rearrange("p (b t) -> p b t", b=2)
        total = small[:, 92:100].rearrange("p (b t) -> p b t", b=2)
        inv = small[:, 100:108].rearrange("p (b t) -> p b t", b=2)
        b_sp = small[:, 108:116]
        norm_b = small[:, 116:120]
        ss_2, ms_2, rs_2 = small[:, 120:124], small[:, 124:128], small[:, 128:132]
        ss_3 = small[:, 132:140].rearrange("p (t n) -> p t n", n=2)
        ms_3 = small[:, 140:148].rearrange("p (t n) -> p t n", n=2)
        rs_3 = small[:, 148:152]

        x_landed = [sem(f"x_landed{t}") for t in range(TT)]
        w_landed = [sem(f"w_landed{s}") for s in range(RING)]
        mix_landed = sem("mix_landed")
        ffn_landed = sem("ffn_landed")
        final_landed = sem("final_landed")
        rel_landed = sem("rel_landed")
        bsp_landed = sem("bsp_landed")
        nb_landed = sem("nb_landed")
        wsp_landed = sem("wsp_landed")
        lng_landed = sem("lng_landed")
        lnb_landed = sem("lnb_landed")
        na_landed = sem("na_landed")
        rel_stored = sem("rel_stored")
        bias_landed = [sem(f"bias_landed{f}") for f in range(HEADS // 2)]
        out_landed = sem("out_landed")

        side_landed = [sem(f"side_landed{i}") for i in range(4)]
        side_hi_ready = sem("side_hi_ready")
        gate_lo_ready = sem("gate_lo_ready")
        up_lo_ready = sem("up_lo_ready")
        first_lo_ready = sem("first_lo_ready")
        w_hi_ready = sem("w_hi_ready")
        w_lo_ready = sem("w_lo_ready")
        w_used = sem("w_used")
        const_step = sem("const_step")
        const_ready = sem("const_ready")
        rel_ready = sem("rel_ready")
        wsp_masked = sem("wsp_masked")
        ss_ready = sem("ss_ready")
        ms_ready = sem("ms_ready")
        rs_ready = sem("rs_ready")
        hn_ready = sem("hn_ready")
        hn_turned = sem("hn_turned")
        h_hi_ready = sem("h_hi_ready")
        h_lo_ready = sem("h_lo_ready")
        proj_done = sem("proj_done")
        wsp_turned = sem("wsp_turned")
        wt_hi_ready = sem("wt_hi_ready")
        wt_lo_ready = sem("wt_lo_ready")
        z_gelu = sem("z_gelu")
        u_gelu = sem("u_gelu")
        z_stats = sem("z_stats")
        z_var = sem("z_var")
        z_ms = sem("z_ms")
        z_rs = sem("z_rs")
        z_step = sem("z_step")
        zn_hi_ready = sem("zn_hi_ready")
        zn_lo_ready = sem("zn_lo_ready")
        q_hi_ready = sem("q_hi_ready")
        q_lo_ready = sem("q_lo_ready")
        k_hi_ready = sem("k_hi_ready")
        k_lo_ready = sem("k_lo_ready")
        v_hi_ready = sem("v_hi_ready")
        v_lo_ready = sem("v_lo_ready")
        mixed = sem("mixed")
        ya_raw = sem("ya_raw")
        ya_ss = sem("ya_ss")
        ya_ms = sem("ya_ms")
        ya_rs = sem("ya_rs")
        ya_scaled = sem("ya_scaled")
        ya_turned = sem("ya_turned")
        ya_hi_ready = sem("ya_hi_ready")
        ya_lo_ready = sem("ya_lo_ready")
        pt_zeroed = sem("pt_zeroed")
        scores_done = sem("scores_done")
        logits_ready = sem("logits_ready")
        top_ready = sem("top_ready")
        exp_done = sem("exp_done")
        inv_ready = sem("inv_ready")
        p_ready = sem("p_ready")
        p_turned = sem("p_turned")
        pt_hi_ready = sem("pt_hi_ready")
        pt_lo_ready = sem("pt_lo_ready")
        pv_done = sem("pv_done")
        yb_hi_ready = sem("yb_hi_ready")
        yb_sq = sem("yb_sq")
        yb_sq_added = sem("yb_sq_added")
        yb_lo_ready = sem("yb_lo_ready")
        yb_ss = sem("yb_ss")
        yb_ms = sem("yb_ms")
        yb_rs = sem("yb_rs")
        tile_done = sem("tile_done")
        x_added = sem("x_added")
        gu_done = sem("gu_done")
        silu_ready = sem("silu_ready")
        prod_ready = sem("prod_ready")
        a_hi_ready = sem("a_hi_ready")
        a_lo_ready = sem("a_lo_ready")
        half_ready = sem("half_ready")
        half_mean = sem("half_mean")
        last_rs_ready = sem("last_rs_ready")
        gains_in = sem("gains_in")
        fin_ready = sem("fin_ready")
        fin_last = sem("fin_last")

        block = ctx.enter_context(nc.Block())

        def row(v):
            return v.partition_broadcast(P)

        def w_unit(buf, i):
            return buf[:, i % RING, :]

        def pair(buf, i):
            return w_unit(buf, i).rearrange("p (k n) -> p k n", k=2)

        def quad(buf, i):
            return w_unit(buf, i).rearrange("p (k n) -> p k n", k=4)

        def rows_of(w, r, n, k):
            return w[r:r + k * P, n].rearrange("(k p) n -> p k n", p=P)

        def unit_wait(it, j):
            return it * 12 + (LOOP0 + j + 1)

        def wait_split(eng, i):
            if i < BY_POOL:
                eng.wait_ge(first_lo_ready, i + 1)
            else:
                eng.wait_ge(w_lo_ready, i + 1 - BY_POOL)

        def out_place(j):
            return divmod(j, 4) if j < 8 else ((j - 8) % 2, (j - 8) // 2)

        def out_bank(j):
            return 3 if j < 8 else [4, 5, 6, 7, 3, 4, 5, 6][j - 8]

        def proj_row(i):
            return hn[:, i, :] if i < 2 else hn_more[:, i - 2, :]

        @block.sync
        def _(sp):
            def load(i, src, dst=None):
                if i >= RING:
                    wait_split(sp, i - RING)
                sp.dma_start(pair(w_raw, i) if dst is None else dst, src).then_inc(w_landed[i % RING], 16)

            def load_in(i):
                n = GROUP_COL[i // 4]
                load(i, rows_of(w_in, (i % 4) * 2 * P, slice(n, n + HALF), 2))

            sp.dma_start(xres[:, 0, :], x[0:P, :]).then_inc(x_landed[0], 16)
            sp.dma_start(gain[:, :], row(norm_mix)).then_inc(mix_landed, 16)
            sp.dma_start(xres[:, 1, :], x[P:2 * P, :]).then_inc(x_landed[1], 16)
            load_in(0)
            sp.dma_start(xres[:, 2, :], x[2 * P:3 * P, :]).then_inc(x_landed[2], 16)
            sp.dma_start(xres[:, 3, :], x[3 * P:4 * P, :]).then_inc(x_landed[3], 16)
            for i in range(1, RING):
                load_in(i)
            sp.dma_start(wsp_raw, w_spatial.rearrange("g t s -> t g s")).then_inc(wsp_landed, 16)
            for i in range(RING, NIN):
                load_in(i)
            for i in range(NOUT):
                r, n = OUT_AT[i]
                load(NIN + i, rows_of(w_out, r, slice(n, n + HALF), 2))

            for i in range(4):
                sp.wait_ge(logits_ready, 8 * i + 8)
                sp.dma_start(side_raw[i].rearrange("p (k n) -> p k n", k=4),
                             rows_of(w_gate if i < 2 else w_up, (i % 2) * 4 * P, slice(0, CHUNK), 4))\
                  .then_inc(side_landed[i], 16)

            with sp.Fori(0, (CHUNKS - 1) // 2) as it:
                for cc in range(2):
                    cols = bass.ds((it * 2 + 1 + cc) * CHUNK, CHUNK)
                    for j in range(6):
                        i = 6 * cc + j
                        sp.wait_ge(w_lo_ready, unit_wait(it, i - RING - BY_POOL))
                        if j < 4:
                            w = w_gate if j < 2 else w_up
                            sp.dma_start(quad(w_raw, LOOP0 + i), rows_of(w, (j % 2) * 4 * P, cols, 4))\
                              .then_inc(w_landed[(LOOP0 + i) % RING], 16)
                        else:
                            r = (it * 2 + cc) * CHUNK + (j - 4) * P
                            sp.dma_start(w_unit(w_raw, LOOP0 + i), w_down[bass.ds(r, P), :])\
                              .then_inc(w_landed[(LOOP0 + i) % RING], 16)
            last = LOOP0 + 6 * (CHUNKS - 1)
            for j in range(2):
                r = (CHUNKS - 1) * CHUNK + j * P
                load(last + j, w_down[r:r + P, :], w_unit(w_raw, last + j))
            for j in range(2 * TT):
                t, n = j // 2, slice(j % 2 * HALF, (j % 2 + 1) * HALF)
                if j < 2 * TT - 1:
                    sp.wait_ge(fin_ready, j + 1)
                else:
                    sp.wait_ge(fin_last, 1)
                src = xres[:, t, n] if t < TT - 1 else last_row[:, n]
                sp.dma_start(out[t * P:(t + 1) * P, n], src).then_inc(out_landed, 16)
            sp.wait_ge(out_landed, 16 * 2 * TT)

        @block.gpsimd
        def _(pool):
            pool.memset(ident[:, :], 0.0).then_inc(const_step, 1)
            pool.memset(half, -0.5).then_inc(const_step, 1)
            pool.memset(ones[:, :], 1.0).then_inc(const_step, 1)
            pool.wait_ge(const_step, 3)
            pool.affine_select(out=ident[:, :], in_=ident[:, :], compare_op=ALU.not_equal, fill=1.0, base=0,
                               pattern=[[-1, P]], channel_multiplier=1).then_inc(const_ready, 1)

            def power(ss, ms, rs, ready, n, ms_sem, rs_sem, at, width):
                pool.wait_ge(ready, n)
                pool.tensor_scalar(ms, ss, 1.0 / width, EPS, ALU.mult, ALU.add).then_inc(ms_sem, 1)
                pool.wait_ge(ms_sem, at)
                pool.tensor_tensor(rs, ms, half[:, 0:rs.shape[1]], ALU.pow).then_inc(rs_sem, 1)

            def first_lo(i):
                pool.wait_ge(w_hi_ready, i + 1)
                pool.tensor_tensor(w_unit(w_lo, i), w_unit(w_raw, i), w_unit(w_hi, i).bitcast(F32),
                                   ALU.subtract).then_inc(first_lo_ready, 1)

            for t in range(TT):
                power(ss_x[:, t:t + 1], ms_x[:, t:t + 1], rs_x[:, t:t + 1], ss_ready, t + 1, ms_ready, rs_ready,
                      t + 1, D)
                if t == 1:
                    first_lo(0)
            first_lo(1)

            pool.wait_ge(wsp_landed, 16)
            pool.affine_select(out=wsp_raw, in_=wsp_raw, compare_op=ALU.is_ge, fill=0.0, base=0,
                               pattern=[[0, GROUPS], [-1, P]], channel_multiplier=1).then_inc(wsp_masked, 1)

            pool.wait_ge(hn_turned, TT)
            pool.dma_start(ln_g, row(gmlp_ln_g)).then_inc(lng_landed, 16)
            pool.dma_start(ln_b, row(gmlp_ln_b)).then_inc(lnb_landed, 16)
            pool.dma_start(norm_a, row(out_norm_a)).then_inc(na_landed, 16)

            pool.wait_ge(rel_landed, 16)
            pool.memset(rel_row[:, 0:P - 1], NEG)
            for b, first, final in bucket_runs():
                n = final - first + 1
                step = pool.tensor_copy(rel_row[:, P - 1 + first:P + final],
                                        rel_tab[:, b:b + 1].to_broadcast([HEADS, n]))
            step.then_inc(rel_ready, 1)
            pool.wait_ge(rel_ready, 1)
            pool.dma_start(rel_dram.ap(), rel_row).then_inc(rel_stored, 16)

            for t in range(TT):
                pool.wait_ge(z_var, t + 1)
                pool.tensor_scalar(ms_z[:, t:t + 1], mv_z[:, t, 1:2], EPS, None, ALU.add).then_inc(z_ms, 1)
                pool.wait_ge(z_ms, t + 1)
                pool.tensor_tensor(rs_z[:, t:t + 1], ms_z[:, t:t + 1], half[:, 0:1], ALU.pow).then_inc(z_rs, 1)
            power(ss_a, ms_a, rs_a, ya_ss, TT, ya_ms, ya_rs, 1, HALF)

            pool.wait_ge(rel_stored, 16)
            for f in range(HEADS // 2):
                if f == 0:
                    pool.wait_ge(ya_ss, TT)
                if f == 2:
                    pool.wait_ge(ya_turned, 4)
                src = bass.AP(rel_dram, 2 * f * REL, [[1, P], [REL, 2], [1, SEQ]])
                pool.dma_start(bias[:, 2 * f:2 * f + 2, :], src).then_inc(bias_landed[f], 16)

            for f in range(1, 4):
                if f == 3:
                    for i in range(2):
                        pool.wait_ge(side_hi_ready, i + 1)
                        pool.tensor_tensor(side_lo[i], side_raw[i], side_hi[i].bitcast(F32), ALU.subtract)\
                            .then_inc(gate_lo_ready, 1)
                        if i == 0:
                            pool.wait_ge(gate_lo_ready, 1)
                            pool.dma_start(gain_ffn, row(norm_ffn)).then_inc(ffn_landed, 16)
                pool.wait_ge(yb_sq, 2 * f + 2)
                if f > 1:
                    pool.wait_ge(yb_sq_added, f - 1)
                pool.tensor_tensor(sq_sum, sq_sum, sq_new, ALU.add).then_inc(yb_sq_added, 1)
            pool.wait_ge(yb_ms, 1)
            pool.tensor_tensor(rs_b, ms_b, half, ALU.pow).then_inc(yb_rs, 1)
            pool.wait_ge(yb_ss, 1)
            pool.dma_start(gain[:, :], row(norm_final)).then_inc(final_landed, 16)
            for t in range(TT):
                power(ss_2[:, t:t + 1], ms_2[:, t:t + 1], rs_2[:, t:t + 1], ss_ready, TT + t + 1, ms_ready,
                      rs_ready, TT + t + 1, D)
            for t in range(TT):
                pool.wait_ge(half_ready, 2 * t + 1)
                pool.tensor_scalar(ms_3[:, t, 0:1], ss_3[:, t, 0:1], 1.0 / D, EPS, ALU.mult, ALU.add)\
                    .then_inc(half_mean, 1)
                pool.wait_ge(half_mean, 2 * t + 1)
                pool.wait_ge(half_ready, 2 * t + 2)
                pool.tensor_scalar(ms_3[:, t, 1:2], ss_3[:, t, 1:2], 1.0 / D, ms_3[:, t, 0:1], ALU.mult, ALU.add)\
                    .then_inc(half_mean, 1)
                pool.wait_ge(half_mean, 2 * t + 2)
                pool.tensor_tensor(rs_3[:, t:t + 1], ms_3[:, t, 1:2], half[:, 0:1], ALU.pow)\
                    .then_inc(last_rs_ready, 1)

        @block.scalar
        def _(act):
            act.preload_act_table(ACT.Gelu_apprx_tanh)
            act.dma_start(rel_tab, rel_bias.rearrange("b h -> h b"),
                          allow_slow_non_contiguous=True).then_inc(rel_landed, 16)
            act.dma_start(b_sp, b_spatial.rearrange("g t -> t g"), allow_slow_non_contiguous=True).then_inc(bsp_landed, 16)
            act.dma_start(norm_b, out_norm_b.rearrange("(f p) -> p f", p=P),
                          allow_slow_non_contiguous=True).then_inc(nb_landed, 16)

            def split_hi(i):
                act.wait_ge(w_landed[i % RING], 16 * (i // RING + 1))
                if i >= RING:
                    act.wait_ge(w_used, i - RING + 1)
                act.activation(w_unit(w_hi, i), w_unit(w_raw, i), ACT.Copy).then_inc(w_hi_ready, 1)

            def square_x(t):
                act.wait_ge(x_landed[t], 16)
                act.activation(ps[:, 2 * t:2 * t + 2, :], xres[:, t, :].rearrange("p (b n) -> p b n", b=2),
                               ACT.Square, accum_out=ss_x[:, t:t + 1]).then_inc(ss_ready, 1)

            def h_evac(t, n, bank):
                act.wait_ge(hn_turned, n)
                act.activation(h_hi[:, :, t * P:(t + 1) * P],
                               ps[:, bank:bank + 2, :].rearrange("p b (k s) -> p (b k) s", s=P),
                               ACT.Copy).then_inc(h_hi_ready, 1)

            square_x(0)
            square_x(1)
            split_hi(0)
            h_evac(0, 1, 0)
            square_x(2)
            square_x(3)
            h_evac(1, 2, 2)
            split_hi(1)
            h_evac(2, 3, 4)
            split_hi(2)
            h_evac(3, 4, 6)
            split_hi(3)

            def zn_split(t):
                act.wait_ge(z_step, 2 * t + 2)
                act.activation(zn_hi[:, t, :], z_act[:, t, :], ACT.Copy).then_inc(zn_hi_ready, 1)

            for e in range(1, NIN):
                split_hi(e + RING - 1)
                if e == 3:
                    act.wait_ge(wsp_turned, 1)
                    act.activation(wt_hi, ps[:, 4:6, :].rearrange("p b (g s) -> p (b g) s", s=P),
                                   ACT.Copy).then_inc(wt_hi_ready, 1)
                if 4 <= e < 8:
                    t = e - 4
                    if t == 0:
                        act.wait_ge(rel_stored, 16)
                    act.wait_ge(proj_done, t + 1)
                    act.activation(z_act[:, t, :], ps[:, t, :], ACT.Gelu_apprx_tanh).then_inc(z_gelu, 1)
                    if t > 0:
                        zn_split(t - 1)
                if 8 <= e < 12:
                    t = e - 8
                    if t == 0:
                        zn_split(3)
                    act.wait_ge(proj_done, 4 + t + 1)
                    act.activation(u_act[:, t, :], ps[:, 4 + t, :], ACT.Gelu_apprx_tanh).then_inc(u_gelu, 1)
                if 12 <= e < 16:
                    f = e - 12
                    act.wait_ge(proj_done, 8 + f + 1)
                    act.activation(q_hi[:, f, :], ps[:, f, :], ACT.Copy, scale=HD ** -0.5).then_inc(q_hi_ready, 1)
                if e == 16:
                    for f in range(4):
                        act.wait_ge(proj_done, 12 + f + 1)
                        act.activation(k_hi[:, f, :], ps[:, 4 + f, :], ACT.Copy).then_inc(k_hi_ready, 1)
                if e == 17:
                    act.wait_ge(ya_raw, GROUPS)
                    for c in range(TT):
                        act.activation(u_act[:, c, :], z_act[:, c, :], ACT.Square,
                                       accum_out=ss_a[:, c:c + 1]).then_inc(ya_ss, 1)
                if e == 19:
                    for f in range(4):
                        act.wait_ge(ya_turned, f + 1)
                        act.activation(ya_hi[:, f, :], ps[:, 4 + f, :], ACT.Copy).then_inc(ya_hi_ready, 1)

            def v_evac(t):
                act.wait_ge(proj_done, 16 + t + 1)
                act.activation(v_hi[:, t, :], ps[:, t, :], ACT.Copy).then_inc(v_hi_ready, 1)

            v_evac(0)
            v_evac(1)

            def side_split(i):
                act.wait_ge(side_landed[i], 16)
                if i < 2:
                    act.wait_ge(scores_done, 16 * (i + 1))
                else:
                    act.wait_ge(tile_done, 8)
                act.activation(side_hi[i], side_raw[i], ACT.Copy).then_inc(side_hi_ready, 1)

            def turned_hi(h, kt):
                b = h % 2
                act.wait_ge(p_turned, 4 * h + kt + 1)
                if h >= 2:
                    act.wait_ge(pv_done, h - 1)
                n = (TT - kt) * P
                at = b * PT_ALL + PT_AT[kt] + kt * P - PT_Q0[kt]
                act.activation(pt_hi[:, at:at + n], ps[:, kt % 2, kt * P:SEQ], ACT.Copy).then_inc(pt_hi_ready, 1)

            def yb_evac(h):
                r, f = (h % 2) * HD, h // 2
                act.wait_ge(pv_done, h + 1)
                if h == 0:
                    act.wait_ge(nb_landed, 16)
                act.activation(yb_hi[r:r + HD, f, :], ps[r:r + HD, 2, :], ACT.Copy,
                               scale=norm_b[r:r + HD, f:f + 1]).then_inc(yb_hi_ready, 1)
                if f > 1:
                    act.wait_ge(yb_sq_added, f - 1)
                dst = sq_new if f else sq_sum
                act.activation(dst[r:r + HD, :], ps[r:r + HD, 2, :], ACT.Square).then_inc(yb_sq, 1)

            def exp_row(s, t):
                b = s % 2
                p_t = prob[:, b, P_AT[t]:P_AT[t] + (t + 1) * P]
                act.activation(p_t, p_t, ACT.Exp, bias=neg_top[:, b, t:t + 1],
                               accum_out=total[:, b, t:t + 1]).then_inc(exp_done, 1)

            for s in range(HEADS + 2):
                if 0 <= s - 1 < HEADS:
                    turned_hi(s - 1, 0)
                    turned_hi(s - 1, 1)
                if s == 3:
                    split_hi(23)
                if s == 5:
                    split_hi(24)
                if s == 6:
                    split_hi(25)
                if s == 7:
                    side_split(0)
                if s < HEADS:
                    act.wait_ge(top_ready, s + 1)
                    for t in range(3):
                        exp_row(s, t)
                if 0 <= s - 1 < HEADS:
                    turned_hi(s - 1, 2)
                    turned_hi(s - 1, 3)
                if s < HEADS:
                    exp_row(s, 3)
                if s == 0:
                    v_evac(3)
                    v_evac(2)
                if s == 8:
                    split_hi(26)
                    split_hi(27)
                if s >= 2:
                    yb_evac(s - 2)
                if s == 8:
                    side_split(1)

            side_split(2)
            side_split(3)
            for t in range(TT):
                if t == 2:
                    h_evac(0, TT + 1, 0)
                    h_evac(1, TT + 2, 2)
                act.wait_ge(x_added, 8 + 2 * t + 2)
                if t >= 2:
                    act.wait_ge(hn_turned, TT + t - 1)
                act.activation(hn[:, t % 2, :], xres[:, t, :], ACT.Square,
                               accum_out=ss_2[:, t:t + 1]).then_inc(ss_ready, 1)
            split_hi(LOOP0)
            split_hi(LOOP0 + 1)
            h_evac(2, TT + 3, 0)
            h_evac(3, TT + 4, 2)

            def ffn(c, it, cc):
                def split_c(j):
                    i = LOOP0 + 6 * cc + j
                    if it is None:
                        split_hi(i)
                        return
                    act.wait_ge(w_landed[i % RING], (it * 3 + (i // RING + 1)) * 16)
                    act.wait_ge(w_used, unit_wait(it, 6 * cc + j - RING))
                    act.activation(w_unit(w_hi, i), w_unit(w_raw, i), ACT.Copy).then_inc(w_hi_ready, 1)

                par = (1 + cc) % 2
                banks = BANK0 if it is None else range(4)
                if it is not None:
                    split_c(2)
                    split_c(3)
                for f in range(2):
                    act.wait_ge(gu_done, c * 4 + (f + 1))
                    act.activation(silu[:, f, :], ps[:, banks[f], :], ACT.Silu).then_inc(silu_ready, 1)
                if it is not None:
                    split_c(4)
                    split_c(5)
                for f in range(2):
                    act.wait_ge(prod_ready, c * 2 + (f + 1))
                    if it is not None:
                        act.wait_ge(tile_done, (c - 1) * 8 + 16)
                    act.activation(act_hi[:, 2 * par + f, :], prod[:, f, :], ACT.Copy).then_inc(a_hi_ready, 1)
                if it is not None:
                    split_c(6)
                    split_c(7)

            ffn(0, None, -1)
            with act.Fori(0, (CHUNKS - 1) // 2) as it:
                for cc in range(2):
                    ffn(it * 2 + (1 + cc), it, cc)
            for j in range(2 * TT):
                t, n = j // 2, slice(j % 2 * HALF, (j % 2 + 1) * HALF)
                act.wait_ge(x_added, 16 + 8 * (CHUNKS - 1) + j + 1)
                if j >= 4:
                    act.wait_ge(half_ready, j - 3)
                act.activation(hn[:, t % 2, n], xres[:, t, n], ACT.Square,
                               accum_out=ss_3[:, t, j % 2:j % 2 + 1]).then_inc(half_ready, 1)
            act.wait_ge(gains_in, 1)
            act.wait_ge(last_rs_ready, TT)
            act.activation(last_row[:, HALF:D], last_row[:, HALF:D], ACT.Copy, scale=rs_3[:, TT - 1:TT])\
               .then_inc(fin_last, 1)

        @block.vector
        def _(dve):
            def split_lo(i):
                dve.wait_ge(w_hi_ready, i + 1)
                dve.tensor_tensor(w_unit(w_lo, i), w_unit(w_raw, i), w_unit(w_hi, i).bitcast(F32),
                                  ALU.subtract).then_inc(w_lo_ready, 1)

            def norm_rows(t, n, rs, gains, dst):
                dve.wait_ge(rs_ready, n + 1)
                dve.scalar_tensor_tensor(out=dst, in0=xres[:, t, :], scalar=rs[:, t:t + 1], in1=gains,
                                         op0=ALU.mult, op1=ALU.mult).then_inc(hn_ready, 1)

            def h_evac(t, n, bank):
                dve.wait_ge(h_hi_ready, n)
                dve.tensor_tensor(h_lo[:, :, t * P:(t + 1) * P],
                                  ps[:, bank:bank + 2, :].rearrange("p b (k s) -> p (b k) s", s=P),
                                  h_hi[:, :, t * P:(t + 1) * P].bitcast(F32), ALU.subtract)\
                   .then_inc(h_lo_ready, 1)

            dve.wait_ge(mix_landed, 16)
            norm_rows(0, 0, rs_x, gain[:, :], proj_row(0))
            norm_rows(1, 1, rs_x, gain[:, :], proj_row(1))
            h_evac(0, 1, 0)
            norm_rows(2, 2, rs_x, gain[:, :], proj_row(2))
            h_evac(1, 2, 2)
            norm_rows(3, 3, rs_x, gain[:, :], proj_row(3))
            h_evac(2, 3, 4)
            h_evac(3, 4, 6)
            split_lo(2)
            split_lo(3)

            def zn_split(t):
                dve.wait_ge(zn_hi_ready, t + 1)
                dve.tensor_tensor(zn_lo[:, t, :], z_act[:, t, :], zn_hi[:, t, :].bitcast(F32),
                                  ALU.subtract).then_inc(zn_lo_ready, 1)

            def layer_norm(t):
                dve.wait_ge(z_gelu, t + 1)
                dve.bn_stats(st_z[:, t, :], z_act[:, t, :]).then_inc(z_stats, 1)
                dve.wait_ge(z_stats, t + 1)
                dve.bn_aggr(mv_z[:, t, :], st_z[:, t, :]).then_inc(z_var, 1)
                if t == 0:
                    dve.wait_ge(lng_landed, 16)
                    dve.wait_ge(lnb_landed, 16)
                dve.wait_ge(z_rs, t + 1)
                dve.scalar_tensor_tensor(out=z_act[:, t, :], in0=z_act[:, t, :], scalar=mv_z[:, t, 0:1], in1=ln_g,
                                         op0=ALU.subtract, op1=ALU.mult).then_inc(z_step, 1)
                dve.wait_ge(z_step, 2 * t + 1)
                dve.scalar_tensor_tensor(out=z_act[:, t, :], in0=z_act[:, t, :], scalar=rs_z[:, t:t + 1], in1=ln_b,
                                         op0=ALU.mult, op1=ALU.add).then_inc(z_step, 1)

            for e in range(1, NIN):
                split_lo(e + RING - 1)
                if e == 3:
                    dve.wait_ge(wt_hi_ready, 1)
                    dve.tensor_tensor(wt_lo, ps[:, 4:6, :].rearrange("p b (g s) -> p (b g) s", s=P),
                                      wt_hi.bitcast(F32), ALU.subtract).then_inc(wt_lo_ready, 1)
                if 4 <= e < 8:
                    layer_norm(e - 4)
                    if e > 4:
                        zn_split(e - 5)
                if e == 8:
                    zn_split(3)
                if 12 <= e < 16:
                    f = e - 12
                    dve.wait_ge(q_hi_ready, f + 1)
                    dve.scalar_tensor_tensor(out=q_lo[:, f, :], in0=ps[:, f, :], scalar=HD ** -0.5,
                                             in1=q_hi[:, f, :].bitcast(F32), op0=ALU.mult, op1=ALU.subtract)\
                       .then_inc(q_lo_ready, 1)
                if e == 16:
                    for f in range(4):
                        dve.wait_ge(k_hi_ready, f + 1)
                        dve.tensor_tensor(k_lo[:, f, :], ps[:, 4 + f, :], k_hi[:, f, :].bitcast(F32),
                                          ALU.subtract).then_inc(k_lo_ready, 1)
                if e == 17:
                    dve.wait_ge(bsp_landed, 16)
                    dve.wait_ge(u_gelu, TT)
                    for g in range(GROUPS):
                        dve.wait_ge(mixed, g // 2 + 1)
                        at = slice(g * GD, (g + 1) * GD)
                        dve.scalar_tensor_tensor(
                            out=z_act[:, :, at],
                            in0=ps[:, 4 + g // 2, (g % 2) * 256:(g % 2 + 1) * 256].rearrange("p (c d) -> p c d", d=GD),
                            scalar=b_sp[:, g:g + 1], in1=u_act[:, :, at], op0=ALU.add, op1=ALU.mult)\
                           .then_inc(ya_raw, 1)
                if e == 18:
                    dve.wait_ge(na_landed, 16)
                    dve.wait_ge(ya_rs, 1)
                    for c in range(TT):
                        dve.scalar_tensor_tensor(out=z_act[:, c, :], in0=z_act[:, c, :], scalar=rs_a[:, c:c + 1],
                                                 in1=norm_a, op0=ALU.mult, op1=ALU.mult).then_inc(ya_scaled, 1)
                if e == 19:
                    for f in range(4):
                        dve.wait_ge(ya_hi_ready, f + 1)
                        dve.tensor_tensor(ya_lo[:, f, :], ps[:, 4 + f, :], ya_hi[:, f, :].bitcast(F32),
                                          ALU.subtract).then_inc(ya_lo_ready, 1)

            def v_evac(t, n):
                dve.wait_ge(v_hi_ready, n)
                dve.tensor_tensor(v_lo[:, t, :], ps[:, t, :], v_hi[:, t, :].bitcast(F32),
                                  ALU.subtract).then_inc(v_lo_ready, 1)

            v_evac(0, 1)
            v_evac(1, 2)

            def add_tile(j):
                n, t = out_place(j)
                dve.wait_ge(tile_done, j + 1)
                dst = xres[:, t, n * HALF:(n + 1) * HALF]
                if j < 8:
                    dve.tensor_tensor(dst, ps[:, 3, :], dst, ALU.add).then_inc(x_added, 1)
                else:
                    if j == 8:
                        dve.wait_ge(yb_rs, 1)
                    dve.wait_ge(x_added, 8)
                    dve.scalar_tensor_tensor(out=dst, in0=ps[:, out_bank(j), :], scalar=rs_b[:, t:t + 1], in1=dst,
                                             op0=ALU.mult, op1=ALU.add).then_inc(x_added, 1)

            def turned_lo(h, kt):
                n = (TT - kt) * P
                at = (h % 2) * PT_ALL + PT_AT[kt] + kt * P - PT_Q0[kt]
                dve.wait_ge(pt_hi_ready, 4 * h + kt + 1)
                dve.tensor_tensor(pt_lo[:, at:at + n], ps[:, kt % 2, kt * P:SEQ], pt_hi[:, at:at + n].bitcast(F32),
                                  ALU.subtract).then_inc(pt_lo_ready, 1)

            def yb_evac(h):
                r, f = slice((h % 2) * HD, (h % 2 + 1) * HD), h // 2
                dve.wait_ge(yb_sq, h + 1)
                dve.scalar_tensor_tensor(out=yb_lo[r, f, :], in0=ps[r, 2, :], scalar=norm_b[r, f:f + 1],
                                         in1=yb_hi[r, f, :].bitcast(F32), op0=ALU.mult, op1=ALU.subtract)\
                   .then_inc(yb_lo_ready, 1)

            for s in range(HEADS + 2):
                if s < HEADS:
                    b = s % 2
                    dve.wait_ge(bias_landed[s // 2], 16)
                    if s >= 2:
                        dve.wait_ge(p_turned, 4 * (s - 1))
                    for t in range(TT):
                        n = (t + 1) * P
                        dve.wait_ge(scores_done, 4 * s + t + 1)
                        dve.tensor_tensor_reduce(out=prob[:, b, P_AT[t]:P_AT[t] + n], in0=ps[:, 4 + t, 0:n],
                                                 in1=bias[:, s, 0:n][:, ::-1], scale=1.0, scalar=-3e38,
                                                 op0=ALU.add, op1=ALU.max, accum_out=top[:, b, t:t + 1])\
                           .then_inc(logits_ready, 1)
                    dve.wait_ge(logits_ready, 4 * s + 4)
                    dve.tensor_scalar(neg_top[:, b, :], top[:, b, :], -1.0, None, ALU.mult).then_inc(top_ready, 1)
                if 0 <= s - 1 < HEADS:
                    turned_lo(s - 1, 0)
                    turned_lo(s - 1, 1)
                    if s >= 3:
                        yb_evac(s - 3)
                    add_tile(s - 1)
                    if s == 1:
                        for bb in range(2):
                            for buf in (pt_hi, pt_lo):
                                at = bb * PT_ALL + PT_AT[3]
                                dve.memset(buf[:, at:at + P].bitcast(F32), 0.0).then_inc(pt_zeroed, 1)
                    if s == 3:
                        split_lo(23)
                    if s == 5:
                        split_lo(24)
                    if s == 6:
                        split_lo(25)
                    turned_lo(s - 1, 2)
                    turned_lo(s - 1, 3)
                if s < HEADS:
                    b = s % 2
                    dve.wait_ge(exp_done, 4 * s + 4)
                    dve.reciprocal(inv[:, b, :], total[:, b, :]).then_inc(inv_ready, 1)
                    dve.wait_ge(inv_ready, s + 1)
                    for t in range(TT):
                        p_t = prob[:, b, P_AT[t]:P_AT[t] + (t + 1) * P]
                        dve.tensor_scalar(p_t, p_t, inv[:, b, t:t + 1], None, ALU.mult).then_inc(p_ready, 1)
                if s == 0:
                    v_evac(3, 3)
                    v_evac(2, 4)
                if s == 8:
                    split_lo(26)
                    split_lo(27)
                if s >= HEADS:
                    yb_evac(s - 2)

            def up_split(i):
                dve.wait_ge(side_hi_ready, i + 1)
                dve.tensor_tensor(side_lo[i], side_raw[i], side_hi[i].bitcast(F32), ALU.subtract)\
                    .then_inc(up_lo_ready, 1)

            up_split(2)
            dve.wait_ge(yb_ss, 1)
            dve.tensor_scalar(ms_b, ps[:, 0, 0:TT], 1.0 / HALF, EPS, ALU.mult, ALU.add).then_inc(yb_ms, 1)
            up_split(3)
            for j in range(8, 13):
                add_tile(j)
            dve.wait_ge(ffn_landed, 16)
            norm_rows(0, TT, rs_2, gain_ffn, hn[:, 0, :])
            norm_rows(1, TT + 1, rs_2, gain_ffn, hn[:, 1, :])
            add_tile(13)
            add_tile(14)
            h_evac(0, TT + 1, 0)
            h_evac(1, TT + 2, 2)
            norm_rows(2, TT + 2, rs_2, gain_ffn, hn[:, 0, :])
            add_tile(15)
            norm_rows(3, TT + 3, rs_2, gain_ffn, hn[:, 1, :])
            h_evac(2, TT + 3, 0)
            h_evac(3, TT + 4, 2)
            split_lo(LOOP0)
            split_lo(LOOP0 + 1)

            def ffn(c, it, cc):
                def split_c(j):
                    i = LOOP0 + 6 * cc + j
                    if it is None:
                        split_lo(i)
                        return
                    dve.wait_ge(w_hi_ready, unit_wait(it, 6 * cc + j))
                    dve.tensor_tensor(w_unit(w_lo, i), w_unit(w_raw, i), w_unit(w_hi, i).bitcast(F32),
                                      ALU.subtract).then_inc(w_lo_ready, 1)

                par = (1 + cc) % 2
                banks = BANK0 if it is None else range(4)
                if it is not None:
                    split_c(2)
                    split_c(3)
                    split_c(4)
                    split_c(5)
                for f in range(2):
                    dve.wait_ge(gu_done, c * 4 + (3 + f))
                    dve.wait_ge(silu_ready, c * 2 + (f + 1))
                    dve.tensor_tensor(prod[:, f, :], silu[:, f, :], ps[:, banks[2 + f], :], ALU.mult)\
                       .then_inc(prod_ready, 1)
                for f in range(2):
                    dve.wait_ge(a_hi_ready, c * 2 + (f + 1))
                    dve.tensor_tensor(act_lo[:, 2 * par + f, :], prod[:, f, :],
                                      act_hi[:, 2 * par + f, :].bitcast(F32), ALU.subtract).then_inc(a_lo_ready, 1)
                if it is not None:
                    split_c(6)
                    add_down(c - 1, 0)
                    split_c(7)
                    for j in range(1, 8):
                        add_down(c - 1, j)

            def add_down(c, j):
                t, n = j // 2, j % 2
                dst = xres[:, t, n * HALF:(n + 1) * HALF]
                dve.wait_ge(tile_done, c * 8 + (17 + j))
                dve.wait_ge(x_added, c * 8 + (9 + j))
                dve.tensor_tensor(dst, ps[:, 4 + j % 4, :], dst, ALU.add).then_inc(x_added, 1)

            ffn(0, None, -1)
            with dve.Fori(0, (CHUNKS - 1) // 2) as it:
                for cc in range(2):
                    ffn(it * 2 + (1 + cc), it, cc)
            dve.wait_ge(final_landed, 16)

            def last_rows(t):
                dve.wait_ge(last_rs_ready, t + 1)
                for n in (slice(0, HALF), slice(HALF, D)):
                    dve.scalar_tensor_tensor(out=xres[:, t, n], in0=xres[:, t, n], scalar=rs_3[:, t:t + 1],
                                             in1=gain[:, n], op0=ALU.mult, op1=ALU.mult).then_inc(fin_ready, 1)

            for t in range(TT):
                add_down(CHUNKS - 1, 2 * t)
                add_down(CHUNKS - 1, 2 * t + 1)
                if t > 0:
                    last_rows(t - 1)
                if t == TT - 1:
                    dve.wait_ge(x_added, 16 + 8 * CHUNKS)
                    dve.tensor_tensor(last_row, xres[:, t, :], gain[:, :], ALU.mult).then_inc(gains_in, 1)
            dve.wait_ge(gains_in, 1)
            dve.wait_ge(last_rs_ready, TT)
            dve.tensor_scalar(last_row[:, 0:HALF], last_row[:, 0:HALF], rs_3[:, TT - 1:TT], None, ALU.mult)\
               .then_inc(fin_ready, 1)

        @block.tensor
        def _(pe):
            def mm3(dst, a, b, at, start, stop, frees=False):
                (a_hi, a_lo), (b_hi, b_lo) = a, b
                sa, sbb = at
                first = pe.matmul(dst, a_hi[sa], b_hi[sbb], start=start, stop=False)
                if frees:
                    first.then_inc(w_used, 1)
                pe.matmul(dst, a_hi[sa], b_lo[sbb], start=False, stop=False)
                return pe.matmul(dst, a_lo[sa], b_hi[sbb], start=False, stop=stop)

            H, W = (h_hi, h_lo), (w_hi, w_lo)
            everything = slice(None)

            def w2(i):
                return pair(w_hi, i), pair(w_lo, i)

            def turn_rows(rows, n, bank):
                pe.wait_ge(hn_ready, n)
                for k in range(KT):
                    last = pe.transpose(ps[:, bank + k // 4, (k % 4) * P:(k % 4 + 1) * P],
                                        rows[:, k * P:(k + 1) * P], ident[:, :])
                last.then_inc(hn_turned, 1)

            pe.wait_ge(const_ready, 1)
            def scores(h):
                f, r = h // 2, slice((h % 2) * HD, (h % 2 + 1) * HD)
                for t in range(TT):
                    if h == 0:
                        pe.wait_ge(ya_lo_ready, t + 1)
                    else:
                        pe.wait_ge(logits_ready, 4 * (h - 1) + t + 1)
                    n = max((t + 1) * P, 256)
                    mm3(ps[:, 4 + t, 0:n], (q_hi, q_lo), (k_hi, k_lo),
                        ((r, f, slice(t * P, (t + 1) * P)), (r, f, slice(0, n))), True, True, h == 1 and t == 0)\
                        .then_inc(scores_done, 1)

            def project(i, m):
                group, j = divmod(i, 4)
                for kk in range(2):
                    w, h = (everything, kk), (everything, 2 * j + kk)
                    if group in (2, 3):
                        ops = w2(i), H, (w + (slice(m * P, (m + 1) * P),), h)
                    else:
                        ops = H, w2(i), (h + (slice(m * P, (m + 1) * P),), w)
                    last = mm3(ps[:, 4 * (group % 2) + m, :], *ops, j == 0 and kk == 0, j == 3 and kk == 1,
                               i > 0 and j == 0 and m == 0 and kk == 0)
                return last

            turn_rows(proj_row(0), 1, 0)
            turn_rows(proj_row(1), 2, 2)
            pe.wait_ge(first_lo_ready, 1)
            pe.wait_ge(h_lo_ready, 1)
            project(0, 0)
            turn_rows(proj_row(2), 3, 4)
            pe.wait_ge(h_lo_ready, 2)
            project(0, 1)
            turn_rows(proj_row(3), 4, 6)
            pe.wait_ge(first_lo_ready, 2)
            project(1, 0)
            project(1, 1)
            pe.wait_ge(h_lo_ready, 3)
            project(0, 2)
            pe.wait_ge(h_lo_ready, 4)
            project(0, 3).then_inc(w_used, 1)
            project(1, 2)
            project(1, 3).then_inc(w_used, 1)

            for i in range(2, NIN):
                j = i % 4
                if i == 4:
                    pe.wait_ge(wt_lo_ready, 1)
                if i == 8:
                    pe.wait_ge(z_gelu, 4)
                if i == 12:
                    pe.wait_ge(u_gelu, 4)
                if i == 16:
                    pe.wait_ge(q_lo_ready, 4)
                wait_split(pe, i)
                for m in range(4):
                    if i == NIN - 1 and m == 2:
                        scores(0)
                    last = project(i, m)
                    if j == 3:
                        last.then_inc(proj_done, 1)
                if j < 3:
                    last.then_inc(w_used, 1)
                if i == 2:
                    pe.wait_ge(wsp_masked, 1)
                    for g in range(GROUPS):
                        last = pe.transpose(ps[:, 4 + g // 4, (g % 4) * P:(g % 4 + 1) * P], wsp_raw[:, g, :],
                                            ident[:, :])
                    last.then_inc(wsp_turned, 1)
                if i == 16:
                    pe.wait_ge(k_lo_ready, 4)
                    pe.wait_ge(zn_lo_ready, 4)
                    for g in range(GROUPS):
                        last = mm3(ps[:, 4 + g // 2, (g % 2) * 256:(g % 2 + 1) * 256], (wt_hi, wt_lo),
                                   (zn_hi, zn_lo),
                                   ((everything, g), (everything, everything, slice(g * GD, (g + 1) * GD))),
                                   True, True)
                        if g % 2:
                            last.then_inc(mixed, 1)
                if i == 18:
                    pe.wait_ge(ya_scaled, 4)
                    for f in range(4):
                        for c in range(TT):
                            last = pe.transpose(ps[:, 4 + f, c * P:(c + 1) * P], z_act[:, c, f * P:(f + 1) * P],
                                                ident[:, :])
                        last.then_inc(ya_turned, 1)

            def out_tile(j, tiles):
                n, t = out_place(j)
                y = (ya_hi, ya_lo) if j < 8 else (yb_hi, yb_lo)
                first = NIN + 2 * n + (0 if j < 8 else 4)
                bank = out_bank(j)
                if j == 0:
                    pe.wait_ge(v_lo_ready, 3)
                elif j < 8:
                    pe.wait_ge(x_added, j)
                elif j >= 12:
                    pe.wait_ge(x_added, 8 if j == 12 else j - 4)
                for k in tiles:
                    i = first + k // 2
                    wait_split(pe, i)
                    last = mm3(ps[:, bank, :], y, w2(i),
                               ((everything, k, slice(t * P, (t + 1) * P)), (everything, k % 2)), k == 0, k == 3,
                               k == 0 and j == 15)
                    if k == 1 and t == 3:
                        last.then_inc(w_used, 1)
                    if k == 3:
                        last.then_inc(tile_done, 1)

            def turn_prob(h, kt):
                n = 4 * h + kt
                if n == 0:
                    pe.wait_ge(v_lo_ready, 2)
                if n >= 2:
                    pe.wait_ge(pt_lo_ready, n - 1)
                for t in range(kt, TT):
                    pe.wait_ge(p_ready, 4 * h + t + 1)
                    at = P_AT[t] + kt * P
                    last = pe.transpose(ps[:, kt % 2, t * P:(t + 1) * P], prob[:, h % 2, at:at + P], ident[:, :])
                    if h % 4 == 3 and kt == 2 and t == 2:
                        last.then_inc(w_used, 1)
                last.then_inc(p_turned, 1)

            def values(h):
                f, b = h // 2, h % 2
                pe.wait_ge(pt_lo_ready, 4 * h + 4)
                if h == 0:
                    pe.wait_ge(v_lo_ready, 4)
                    pe.wait_ge(pt_zeroed, 4)
                else:
                    pe.wait_ge(yb_lo_ready, h)
                for kt in range(TT):
                    at = b * PT_ALL + PT_AT[kt]
                    n = SEQ - PT_Q0[kt]
                    last = mm3(ps[:, 2, PT_Q0[kt]:SEQ], (v_hi, v_lo), (pt_hi, pt_lo),
                               ((everything, kt, slice(f * P, (f + 1) * P)), (everything, slice(at, at + n))),
                               kt == 0, kt == 3)
                last.then_inc(pv_done, 1)

            for s in range(1, HEADS + 1):
                if s < HEADS:
                    scores(s)
                turn_prob(s - 1, 0)
                turn_prob(s - 1, 1)
                out_tile(s - 1, range(4))
                turn_prob(s - 1, 2)
                turn_prob(s - 1, 3)
                if s >= 2:
                    values(s - 2)

            pe.wait_ge(yb_lo_ready, HEADS - 2)
            for j in range(8, 12):
                out_tile(j, range(3))
            values(HEADS - 1)
            out_tile(12, range(3))
            pe.wait_ge(yb_lo_ready, HEADS)
            out_tile(8, [3])
            out_tile(9, [3])
            pe.wait_ge(yb_sq_added, 3)
            for t in range(TT):
                last = pe.matmul(ps[:, 0, t:t + 1], sq_sum[:, t * P:(t + 1) * P], ones[:, 0:1],
                                 start=True, stop=True)
            last.then_inc(yb_ss, 1)
            for j in range(10, 13):
                out_tile(j, [3])
            out_tile(13, range(4))
            out_tile(14, range(4))
            turn_rows(hn[:, 0, :], TT + 1, 0)
            pe.wait_ge(x_added, 13)
            turn_rows(hn[:, 1, :], TT + 2, 2)
            out_tile(15, range(4))

            def gate_up(parts, f, s, bank, frees, used):
                for k in range(KT):
                    hi, lo = parts[k // 4]
                    last = mm3(ps[:, bank, s], (hi, lo), H,
                               ((everything, k % 4, slice(f * P, (f + 1) * P)), (everything, k, s)),
                               k == 0, k == KT - 1, frees and k == 0)
                    if used and k == 3:
                        last.then_inc(w_used, 1)
                return last

            side = [(a.rearrange("p (k n) -> p k n", k=4), b.rearrange("p (k n) -> p k n", k=4))
                    for a, b in zip(side_hi, side_lo)]
            pe.wait_ge(h_lo_ready, TT + 2)
            for m in range(4):
                pe.wait_ge(x_added, 12 + m if m == 0 else 13 + m)
                if m < 2:
                    pe.wait_ge(gate_lo_ready, 2)
                else:
                    pe.wait_ge(up_lo_ready, 2)
                gate_up(side[2 * (m // 2):], m % 2, slice(0, 256), BANK0[m], False, False)
                if m < 2:
                    pe.wait_ge(h_lo_ready, TT + 1 + m)
                    turn_rows(hn[:, m, :], TT + 3 + m, 2 * m)
            pe.wait_ge(h_lo_ready, TT + 4)
            for m in range(4):
                gate_up(side[2 * (m // 2):], m % 2, slice(256, SEQ), BANK0[m], False, False).then_inc(gu_done, 1)

            def down(c, par, units, ready):
                pe.wait_ge(a_lo_ready, c * 2 + 2)
                ready()
                for j in range(8):
                    t, n = j // 2, j % 2
                    pe.wait_ge(x_added, c * 8 + (13 + j))
                    for f in range(2):
                        i = units + f
                        last = mm3(ps[:, 4 + j % 4, :], (act_hi, act_lo), (w_unit(w_hi, i), w_unit(w_lo, i)),
                                   ((everything, 2 * par + f, slice(t * P, (t + 1) * P)),
                                    (everything, slice(n * HALF, (n + 1) * HALF))), f == 0, f == 1, j + f == 0)
                        if j == 7 and f == 0:
                            last.then_inc(w_used, 1)
                    last.then_inc(tile_done, 1)

            with pe.Fori(0, (CHUNKS - 1) // 2) as it:
                for cc in range(2):
                    c = it * 2 + (1 + cc)
                    for m in range(4):
                        pe.wait_ge(w_lo_ready, unit_wait(it, 6 * cc + 2 * (m // 2) + 1 - BY_POOL))
                        pe.wait_ge(silu_ready if m < 2 else prod_ready, c * 2 - (1 - m % 2))
                        i = LOOP0 + 6 * cc + 2 * (m // 2)
                        gate_up([(quad(w_hi, i), quad(w_lo, i)), (quad(w_hi, i + 1), quad(w_lo, i + 1))],
                                m % 2, slice(0, SEQ), m, m % 2 == 0, m % 2 == 1).then_inc(gu_done, 1)
                    down(c - 1, cc, LOOP0 + 6 * cc + 4,
                         lambda: pe.wait_ge(w_lo_ready, unit_wait(it, 6 * cc + 5 - BY_POOL)))
            last = LOOP0 + 6 * (CHUNKS - 1)
            down(CHUNKS - 1, (CHUNKS - 1) % 2, last, lambda: pe.wait_ge(w_lo_ready, last + 2 - BY_POOL))


_INS = ['x', 'rel_bias', 'norm_mix', 'w_in', 'gmlp_ln_g', 'gmlp_ln_b', 'w_spatial', 'b_spatial', 'out_norm_b',
        'out_norm_a', 'w_out', 'norm_ffn', 'w_gate', 'w_up', 'w_down', 'norm_final']


def kernel(**inputs):
    import numpy as _np
    import concourse.bacc as _bacc
    from concourse import mybir as _mybir
    from concourse.bass_utils import run_bass_kernel_spmd as _run

    nc = _bacc.Bacc("TRN2", target_bir_lowering=False, num_devices=1)
    arrays, args = {}, []
    for name in _INS:
        a = _np.ascontiguousarray(inputs[name])
        if name not in ('rel_bias', 'norm_final'):
            a = a[0]
        a = _np.ascontiguousarray(a)
        arrays[f"in_{name}_dram"] = a
        args.append(nc.dram_tensor(f"in_{name}_dram", a.shape, _mybir.dt.from_np(a.dtype), kind="ExternalInput").ap())
    args.append(nc.dram_tensor("out_dram", (SEQ, D), F32, kind="ExternalOutput").ap())
    hybrid_layer(nc, *args)
    r = _run(nc, [arrays], core_ids=[0])
    return r.results[0]["out_dram"].reshape(1, SEQ, D)
```
